# Optimizing a Trainium2 kernel written in Bass

```python
import functools
import jax, jax.numpy as jnp
from jax import lax
import numpy as np

D_MODEL = 2048
BATCH = 1
SEQ = 256
DEPTH = 1
DEC_BATCH = 8
DEC_SEQ = 1
PAST_LEN = 1024
PAGE_SIZE = 128

H_R = 4
DK_R = 256
DV_R = 256
W_R = H_R * DV_R
CHUNK = 128
ROPE_BASE = 10000.0
GN_EPS = 1e-6
H_F = 8
D_F = 128
W_F = H_F * D_F
Q_BLOCK = 128
D_FF = -(-8 * D_MODEL // (3 * 256)) * 256
D_PLE = 256
LN_EPS = 1e-5
ALPHA = (2.0 * DEPTH) ** 0.25
BETA = (8.0 * DEPTH) ** -0.25
IN_SIZES = (H_R * DK_R, H_R * DK_R, H_R * DV_R, H_R * DV_R, W_F, W_F, W_F, H_F, D_MODEL, D_MODEL)
N_IN = sum(IN_SIZES)

kernel_name = 'hybrid_retention_fox_decoder_step'

def layer_norm(x, g, b):
    xf = x.astype(jnp.float32)
    mu = xf.mean(-1, keepdims=True)
    var = jnp.square(xf - mu).mean(-1, keepdims=True)
    return ((xf - mu) * lax.rsqrt(var + LN_EPS) * g + b).astype(x.dtype)

def rope(x, pos):
    half = x.shape[-1] // 2
    inv = ROPE_BASE ** (-jnp.arange(half, dtype=jnp.float32) / half)
    ang = pos.astype(jnp.float32)[:, None] * inv[None, :]
    cos = jnp.cos(ang)[None, :, None, :]
    sin = jnp.sin(ang)[None, :, None, :]
    x = x.astype(jnp.float32)
    x1, x2 = x[..., :half], x[..., half:]
    return jnp.concatenate([x1 * cos - x2 * sin, x2 * cos + x1 * sin], axis=-1)

def branch_inputs(h, w_in, b_f, pos):
    b, l = h.shape[0], h.shape[1]
    z = h @ w_in
    cuts = [int(c) for c in np.cumsum(IN_SIZES)[:-1]]
    rq, rk, rv, rg, fq, fk, fv, ff, gr, gf = jnp.split(z, cuts, axis=-1)
    rq = rope(rq.reshape(b, l, H_R, DK_R), pos)
    rk = rope(rk.reshape(b, l, H_R, DK_R), pos) * (DK_R ** -0.5)
    rv = rv.reshape(b, l, H_R, DV_R)
    fq = fq.reshape(b, l, H_F, D_F)
    fk = fk.reshape(b, l, H_F, D_F)
    fv = fv.reshape(b, l, H_F, D_F)
    logf = jax.nn.log_sigmoid(ff.astype(jnp.float32) + b_f.astype(jnp.float32))
    return rq, rk, rv, rg, fq, fk, fv, logf, gr, gf

def retention_chunk(q, k, v, state, log_g):
    q = q.astype(jnp.float32)
    k = k.astype(jnp.float32)
    v = v.astype(jnp.float32)
    state = state.astype(jnp.float32)
    l = q.shape[1]
    i = jnp.arange(l, dtype=jnp.float32)
    diff = i[:, None] - i[None, :]
    causal = diff >= 0
    dec = jnp.where(causal[None], jnp.exp(log_g[:, None, None] * jnp.where(causal, diff, 0.0)[None]), 0.0)
    scores = jnp.einsum('bihd,bjhd->bhij', q, k) * dec[None]
    o = jnp.einsum('bhij,bjhe->bihe', scores, v)
    cross = jnp.exp(log_g[None, :] * (i[:, None] + 1.0))
    o = o + jnp.einsum('bihd,bhde->bihe', q, state) * cross[None, :, :, None]
    kdec = jnp.exp(log_g[None, :] * (l - 1.0 - i)[:, None])
    new_state = jnp.exp(log_g * l)[None, :, None, None] * state + jnp.einsum('bjhd,bjhe->bhde', k * kdec[None, :, :, None], v)
    return o, new_state

def retention_prompt(q, k, v, log_g):
    b, s = q.shape[0], q.shape[1]
    nc = s // CHUNK

    def chunks(t):
        return jnp.swapaxes(t.reshape((b, nc, CHUNK) + t.shape[2:]), 0, 1)

    def step(state, qkv):
        o, state = retention_chunk(qkv[0], qkv[1], qkv[2], state, log_g)
        return state, o

    s0 = jnp.zeros((b, H_R, DK_R, DV_R), jnp.float32)
    s_fin, o = lax.scan(step, s0, (chunks(q), chunks(k), chunks(v)))
    return jnp.swapaxes(o, 0, 1).reshape(b, s, H_R, DV_R), s_fin

def fox_prompt(q, k, v, logf):
    b, s = q.shape[0], q.shape[1]
    nb = s // Q_BLOCK
    c_t = jnp.swapaxes(jnp.cumsum(logf, axis=1), 1, 2)
    kpos = jnp.arange(s)
    scale = D_F ** -0.5

    def block(bi):
        start = bi * Q_BLOCK
        qb = lax.dynamic_slice_in_dim(q, start, Q_BLOCK, axis=1)
        cb = lax.dynamic_slice_in_dim(c_t, start, Q_BLOCK, axis=2)
        sc = jnp.einsum('bqhd,bkhd->bhqk', qb, k).astype(jnp.float32) * scale + cb[..., None] - c_t[:, :, None, :]
        qpos = start + jnp.arange(Q_BLOCK)
        sc = jnp.where((kpos[None, :] <= qpos[:, None])[None, None], sc, -jnp.inf)
        p = jax.nn.softmax(sc, axis=-1)
        return jnp.einsum('bhqk,bkhd->bqhd', p.astype(v.dtype), v)

    o = lax.map(block, jnp.arange(nb))
    return jnp.swapaxes(o, 0, 1).reshape(b, s, H_F, D_F)

def fox_sample(q, k_new, v_new, logf_new, k_past, v_past, logf_past):
    p_len, t = k_past.shape[1], q.shape[1]
    c = jnp.cumsum(jnp.concatenate([logf_past.astype(jnp.float32), logf_new.astype(jnp.float32)], axis=1), axis=1)
    c_t = jnp.swapaxes(c, 1, 2)
    c_q = c_t[:, :, p_len:]
    s_past = jnp.einsum('bqhd,bkhd->bhqk', q, k_past).astype(jnp.float32)
    s_new = jnp.einsum('bqhd,bkhd->bhqk', q, k_new).astype(jnp.float32)
    sc = jnp.concatenate([s_past, s_new], axis=-1) * (D_F ** -0.5) + c_q[..., None] - c_t[:, :, None, :]
    mask = jnp.concatenate([jnp.ones((t, p_len), bool), jnp.tril(jnp.ones((t, t), bool))], axis=1)
    sc = jnp.where(mask[None, None], sc, -jnp.inf)
    p = jax.nn.softmax(sc, axis=-1).astype(v_new.dtype)
    return jnp.einsum('bhqk,bkhd->bqhd', p[..., :p_len], v_past) + jnp.einsum('bhqk,bkhd->bqhd', p[..., p_len:], v_new)

def attend_prompt(rq, rk, rv, fq, fk, fv, logf, log_g):
    o_r, s_new = retention_prompt(rq, rk, rv, log_g)
    return o_r, s_new, fox_prompt(fq, fk, fv, logf)

def attend_sample(rq, rk, rv, fq, fk, fv, logf, log_g, state, k_past, v_past, logf_past):
    o_r, s_new = retention_chunk(rq, rk, rv, state, log_g)
    return o_r, s_new, fox_sample(fq, fk, fv, logf, k_past, v_past, logf_past)

def trunk_layer(h, p, pos, attend, w_in, b_f, gn_g, w_ret_proj, w_fox_proj, w_out,
                ln1_g, ln1_b, w1, w3, w2, w_pg, w_pe, ln2_g, ln2_b):
    b, l = h.shape[0], h.shape[1]
    rq, rk, rv, rg, fq, fk, fv, logf, gr, gf = branch_inputs(h, w_in, b_f, pos)
    o_r, s_new, o_f = attend(rq, rk, rv, fq, fk, fv, logf)
    mu = o_r.mean(-1, keepdims=True)
    var = jnp.square(o_r - mu).mean(-1, keepdims=True)
    o_r = (o_r - mu) * lax.rsqrt(var + GN_EPS) * gn_g.astype(jnp.float32) * jax.nn.silu(rg.astype(jnp.float32).reshape(b, l, H_R, DV_R))
    y_r = o_r.reshape(b, l, W_R).astype(h.dtype) @ w_ret_proj
    y_f = o_f.reshape(b, l, W_F).astype(h.dtype) @ w_fox_proj
    mix = (jax.nn.sigmoid(gr) * y_r + jax.nn.sigmoid(gf) * y_f) @ w_out
    x1 = layer_norm(ALPHA * h + mix, ln1_g, ln1_b)
    ffn = (jax.nn.silu(x1 @ w1) * (x1 @ w3)) @ w2
    ple = jax.nn.sigmoid(x1 @ w_pg) * (p.astype(h.dtype) @ w_pe)
    y = layer_norm(ALPHA * x1 + ffn + ple, ln2_g, ln2_b)
    return y, (s_new, fk, fv, logf)

def setup_inputs(seed: int = 0) -> dict:
    key = jax.random.key(seed)
    ks = jax.random.split(key, 32)
    f32 = jnp.float32
    n_pages = PAST_LEN // PAGE_SIZE
    n_pool = (5 * DEC_BATCH * n_pages + 3) // 4

    def nrm(k, shape, scale=1.0):
        return jax.random.normal(k, shape, f32) * scale

    col_scale = np.concatenate([np.full((s,), BETA if i in (2, 6) else 1.0, np.float32) for i, s in enumerate(IN_SIZES)])
    page_table = jax.random.permutation(ks[7], n_pool)[: DEC_BATCH * n_pages].reshape(DEC_BATCH, n_pages).astype(jnp.int32)
    return {
        'x_prompt': nrm(ks[0], (BATCH, SEQ, D_MODEL)),
        'x_sample': nrm(ks[1], (DEC_BATCH, DEC_SEQ, D_MODEL)),
        'state_ret': nrm(ks[2], (DEPTH, DEC_BATCH, H_R, DK_R, DV_R), 0.3),
        'cache_k': nrm(ks[3], (DEPTH, n_pool, PAGE_SIZE, H_F, D_F)),
        'cache_v': nrm(ks[4], (DEPTH, n_pool, PAGE_SIZE, H_F, D_F), BETA),
        'cache_logf': jax.nn.log_sigmoid(2.0 + nrm(ks[5], (DEPTH, n_pool, PAGE_SIZE, H_F))),
        'page_table': page_table,
        'p_prompt': nrm(ks[8], (DEPTH, BATCH, SEQ, D_PLE)),
        'p_sample': nrm(ks[9], (DEPTH, DEC_BATCH, DEC_SEQ, D_PLE)),
        'ln_emb_g': 1.0 + nrm(ks[10], (D_MODEL,), 0.02),
        'ln_emb_b': nrm(ks[11], (D_MODEL,), 0.02),
        'w_in': nrm(ks[12], (DEPTH, D_MODEL, N_IN), D_MODEL ** -0.5) * jnp.asarray(col_scale),
        'b_f': 2.0 + nrm(ks[13], (DEPTH, H_F), 0.1),
        'gn_g': 1.0 + nrm(ks[14], (DEPTH, H_R, DV_R), 0.02),
        'w_ret_proj': nrm(ks[15], (DEPTH, W_R, D_MODEL), BETA * W_R ** -0.5),
        'w_fox_proj': nrm(ks[16], (DEPTH, W_F, D_MODEL), BETA * W_F ** -0.5),
        'w_out': nrm(ks[17], (DEPTH, D_MODEL, D_MODEL), BETA * D_MODEL ** -0.5),
        'ln1_g': 1.0 + nrm(ks[18], (DEPTH, D_MODEL), 0.02),
        'ln1_b': nrm(ks[19], (DEPTH, D_MODEL), 0.02),
        'w1': nrm(ks[20], (DEPTH, D_MODEL, D_FF), BETA * D_MODEL ** -0.5),
        'w3': nrm(ks[21], (DEPTH, D_MODEL, D_FF), BETA * D_MODEL ** -0.5),
        'w2': nrm(ks[22], (DEPTH, D_FF, D_MODEL), BETA * D_FF ** -0.5),
        'w_pg': nrm(ks[23], (DEPTH, D_MODEL, D_MODEL), D_MODEL ** -0.5),
        'w_pe': nrm(ks[24], (DEPTH, D_PLE, D_MODEL), BETA * D_PLE ** -0.5),
        'ln2_g': 1.0 + nrm(ks[25], (DEPTH, D_MODEL), 0.02),
        'ln2_b': nrm(ks[26], (DEPTH, D_MODEL), 0.02),
    }

def reference(x_prompt, x_sample, state_ret, cache_k, cache_v, cache_logf, page_table, p_prompt, p_sample,
              ln_emb_g, ln_emb_b, w_in, b_f, gn_g, w_ret_proj, w_fox_proj, w_out, ln1_g, ln1_b,
              w1, w3, w2, w_pg, w_pe, ln2_g, ln2_b):
    dec_b, n_pages = page_table.shape
    past_len = n_pages * PAGE_SIZE
    pos_p = jnp.arange(x_prompt.shape[1])
    pos_s = past_len + jnp.arange(x_sample.shape[1])
    log_g = jnp.log1p(-jnp.exp2(-5.0 - jnp.arange(H_R, dtype=jnp.float32)))
    h_p = layer_norm(x_prompt, ln_emb_g, ln_emb_b)
    h_s = layer_norm(x_sample, ln_emb_g, ln_emb_b)
    outs_p = []
    outs_s = []
    for l in range(DEPTH):
        weights = (w_in[l], b_f[l], gn_g[l], w_ret_proj[l], w_fox_proj[l], w_out[l], ln1_g[l], ln1_b[l],
                   w1[l], w3[l], w2[l], w_pg[l], w_pe[l], ln2_g[l], ln2_b[l])
        h_p, st_p = trunk_layer(h_p, p_prompt[l], pos_p, functools.partial(attend_prompt, log_g=log_g), *weights)
        k_past = cache_k[l][page_table].reshape(dec_b, past_len, H_F, D_F)
        v_past = cache_v[l][page_table].reshape(dec_b, past_len, H_F, D_F)
        logf_past = cache_logf[l][page_table].reshape(dec_b, past_len, H_F)
        attend_s = functools.partial(attend_sample, log_g=log_g, state=state_ret[l],
                                     k_past=k_past, v_past=v_past, logf_past=logf_past)
        h_s, st_s = trunk_layer(h_s, p_sample[l], pos_s, attend_s, *weights)
        outs_p.append(st_p)
        outs_s.append(st_s)
    ret_state_prompt = jnp.stack([o[0] for o in outs_p])
    fox_k_prompt = jnp.stack([o[1] for o in outs_p])
    fox_v_prompt = jnp.stack([o[2] for o in outs_p])
    fox_logf_prompt = jnp.stack([o[3] for o in outs_p])
    ret_state_sample = jnp.stack([o[0] for o in outs_s])
    fox_k_sample = jnp.stack([o[1] for o in outs_s])
    fox_v_sample = jnp.stack([o[2] for o in outs_s])
    fox_logf_sample = jnp.stack([o[3] for o in outs_s])
    return (h_p, h_s, ret_state_prompt, fox_k_prompt, fox_v_prompt, fox_logf_prompt,
            ret_state_sample, fox_k_sample, fox_v_sample, fox_logf_sample)


_drawn_inputs = setup_inputs


def setup_inputs(seed=0):
    import zlib

    import numpy as np

    out = dict(_drawn_inputs(seed))
    spreads = {}
    factors = {'cache_logf': 200.0,
     'gn_g': 36.486,
     'ln1_g': 7.888,
     'ln1_b': 8.039,
     'ln2_g': 20.303,
     'ln2_b': 21.58,
     'cache_k': 7.493,
     'cache_v': 3.311,
     'w_pg': 2.748}
    for name, (base, spread) in spreads.items():
        noise = np.random.default_rng([zlib.crc32(name.encode()), seed]).standard_normal(out[name].shape)
        drawn = base * np.exp(spread * noise) if base else spread * noise
        out[name] = __import__('jax').numpy.asarray(drawn.astype(out[name].dtype))
    for name, factor in factors.items():
        out[name] = (out[name] * factor).astype(out[name].dtype)
    return out
```

```python
from contextlib import ExitStack

import numpy as np

import concourse.bass as bass
from concourse import mybir

F32 = mybir.dt.float32
F32R = mybir.dt.float32r
I32 = mybir.dt.int32
ALU = mybir.AluOpType
ACT = mybir.ActivationFunctionType
AX = mybir.AxisListType
ds = bass.ds

P = 128
RING = 4
AHEAD = 3
PAGES = 4
KT = 4
NC = 256
BIG = -1.0e30


def shape_constants(SEQ, DEC, PAST, H_R):
    half = 128
    f = np.float32
    inv = (f(10000.0) ** (-np.arange(half, dtype=f) / f(half))).astype(f)
    pos = np.concatenate([np.arange(SEQ), np.full(DEC, PAST)]).astype(f)
    ang = inv[:, None] * pos[None, :]
    i = np.arange(P)
    le = (i[:, None] <= i[None, :]).astype(f)
    gt = (i[:, None] > i[None, :]).astype(f)
    ones = np.ones((P, P), f)
    causal = np.where(i[None, :] <= i[:, None], 0.0, BIG).astype(f)
    log_g = np.log1p(-np.exp2(-5.0 - np.arange(H_R, dtype=np.float64)))
    scale = 1.0 / 16.0
    j, t = np.arange(P)[:, None], np.arange(SEQ)[None, :]
    dmask = [np.where(t >= j, np.exp(lg * (t - j)) * scale, 0.0) for lg in log_g]
    kdec = [np.exp(lg * (SEQ - 1 - (blk * P + i)))[:, None] * scale for lg in log_g for blk in range(SEQ // P)]
    parts = {
        "ident": np.eye(P), "le": le, "ones": ones, "gt": gt,
        "mask": np.concatenate([causal, np.zeros((P, P)), causal], 1),
        "cos": np.cos(ang), "nsin": -np.sin(ang), "psin": np.sin(ang),
        "dmask": np.concatenate(dmask, 1), "kdec": np.concatenate(kdec, 1),
        "eps": np.tile([[1e-5, 1e-6]], (P, 1)),
    }
    at, where = 0, {}
    for k, a in parts.items():
        where[k] = (at, a.shape[1])
        at += a.shape[1]
    return np.concatenate([np.asarray(a, f) for a in parts.values()], 1).astype(f), where, [float(np.exp(x)) for x in log_g]


class Chunk:

    def __init__(self, src, rhs, kt0, n_kt, acc, first, last, ready=None):
        self.src, self.rhs, self.kt0, self.n_kt = src, rhs, kt0, n_kt
        self.acc, self.first, self.last, self.ready = acc, first, last, ready


class Phase:

    def __init__(self, plan, iters, chunks):
        assert len(chunks) % RING == 0
        self.iters, self.chunks, self.chunk0 = iters, chunks, plan["chunks"]
        self.group0 = list(plan["groups"])
        self.per = [sum(c.first for c in chunks if c.acc == a) for a in (0, 1)]
        plan["chunks"] += iters * len(chunks)
        for a in (0, 1):
            plan["groups"][a] += iters * self.per[a]

    def number(self, it, j):
        return it * len(self.chunks) + (self.chunk0 + j)

    def group(self, it, j):
        acc = self.chunks[j].acc
        before = sum(c.first for c in self.chunks[:j + 1] if c.acc == acc) - 1
        return it * self.per[acc] + (self.group0[acc] + before)

    def n_kt(self, j):
        return self.chunks[j % len(self.chunks)].n_kt


class Chain:

    def __init__(self, eng, sem):
        self.eng, self.sem, self.base, self.n = eng, sem, 0, 0

    def step(self, ins):
        self.n += 1
        ins.then_inc(self.sem, 1)
        self.eng.wait_ge(self.sem, self.base + self.n)

    def enter(self, it, per):
        self.start, self.per = self.base + self.n, per
        self.base, self.n = it * per + self.start, 0

    def leave(self, iters):
        assert self.n <= self.per, self.n
        if self.per > self.n:
            self.eng.sem_inc(self.sem, self.per - self.n)
        self.base, self.n = self.start + iters * self.per, 0


def layer_kernel(nc, a, where, gammas, dims):
    D, SEQ, DEC, NPG, NPOOL, H_R, H_F, D_FF = (dims[k] for k in ("D", "SEQ", "DEC", "NPG", "NPOOL", "H_R", "H_F", "D_FF"))
    T = SEQ + DEC
    DT = D // P
    NB = SEQ // P
    HF2 = D_FF // P // 2
    ALPHA = 2.0 ** 0.25
    QS = float(P) ** -0.5
    assert DT == 16 and NB == 2 and DEC == 8 and NPG == 8 and H_F == 8 and H_R == 4 and HF2 == 22

    ctx = ExitStack()
    with ctx:
        slab_bytes = 212800
        slab = ctx.enter_context(nc.sbuf_tensor("slab", [P, slab_bytes // 4], F32))
        base = SLAB_BASE
        top = [0]
        made = {}

        def place(name, shape, dt, at=None):
            size = int(np.prod(shape[1:])) * 4
            if at is None:
                at, top[0] = top[0], (top[0] + size + 31) // 32 * 32
            assert at % 32 == 0 and at + size <= slab_bytes, (name, at, size)
            made[name] = (at, size)
            return nc.alloc_sbuf_tensor_at(name, shape, dt, offset=base + at)

        def after(name):
            return (made[name][0] + made[name][1] + 31) // 32 * 32

        raw = place("raw", [P, RING, KT, NC], F32)
        whi = place("whi", [P, RING, KT, NC], F32R)
        wlo = place("wlo", [P, RING, KT, NC], F32R)
        hT_hi = place("hT_hi", [P, DT, T], F32R)
        hT_lo = place("hT_lo", [P, DT, T], F32R)
        orT_hi = place("orT_hi", [P, 8, T], F32R)
        orT_lo = place("orT_lo", [P, 8, T], F32R)
        ofT_hi = place("ofT_hi", [P, 8, T], F32R)
        ofT_lo = place("ofT_lo", [P, 8, T], F32R)
        region = top[0]
        gate = place("gate", [P, DT, 2, T], F32)
        stateS = place("stateS", [P, H_R, 2, 256], F32)
        vbc = place("vbc", [P, H_R, 256], F32)
        page = place("page", [P, PAGES, 1024], F32)
        qbc = place("qbc", [P, 1024], F32)
        s8 = place("s8", [8, 1032], F32)
        n_const = sum(w for _, w in where.values())
        cst = place("cst", [P, n_const], F32)
        par = place("par", [P, 104], F32)
        pT_hi = place("pT_hi", [P, 2, T], F32R)
        pT_lo = place("pT_lo", [P, 2, T], F32R)
        bias_past = place("bias_past", [P, DEC, NPG, H_F], F32)
        sc8 = place("sc8", [P, NPG, H_F], F32)
        scd = place("scd", [P, NPG, H_F], F32)
        pagesum = place("pagesum", [P, P], F32)
        probT = place("probT", [P, NPG, H_F], F32)
        qS = place("qS", [P, H_F, DEC], F32)
        kS = place("kS", [P, H_F, DEC], F32)
        vS = place("vS", [P, H_F, DEC], F32)
        ofS = place("ofS", [P, H_F, DEC], F32)
        rqS = place("rqS", [P, H_R, 2, DEC], F32)
        rkS = place("rkS", [P, H_R, 2, DEC], F32)
        sgS = place("sgS", [P, H_R, 2, DEC], F32)
        orS = place("orS", [P, H_R, 2, DEC], F32)
        prodS = place("prodS", [P, DEC, H_F], F32)
        logf_tok = place("logf_tok", [P, NB, H_F], F32)
        lf4 = place("lf4", [P, NB, 4], F32)
        logfS = place("logfS", [8, H_F], F32)
        lfn8 = place("lfn8", [8, DEC], F32)
        snew8 = place("snew8", [8, DEC], F32)
        pnew8 = place("pnew8", [8, DEC], F32)
        pdiag = place("pdiag", [8, H_F, DEC], F32)
        bf = place("bf", [P, H_F], F32)
        ptab = place("ptab", [1, DEC * NPG], I32)
        stat = place("stat", [P, 64], F32)
        small = place("small", [P, 4, 64], F32)
        softs = place("softs", [P, 24], F32)

        def const(name, rows=P):
            at, n = where[name]
            return cst[0:rows, at:at + n]
        ident = const("ident")
        xtok = place("xtok", [P, 3, D], F32, at=region)
        h32 = place("h32", [P, DT, T], F32, at=after("xtok"))
        wff = place("wff", [P, DT, H_F], F32, at=after("h32"))
        ptok = place("ptok", [P, 3, 256], F32, at=after("wff"))
        prow = place("prow", [104, P], F32, at=after("ptok"))
        Lc = place("Lc", [P, DEC * NPG, H_F], F32, at=made["page"][0])
        kT4 = place("kT4", [P, 4, T], F32, at=region)
        qT4 = place("qT4", [P, 4, T], F32, at=after("kT4"))
        vT4 = place("vT4", [P, 4, T], F32, at=after("qT4"))
        ktok = place("ktok", [P, 2, 512], F32, at=after("vT4"))
        kqs = place("kqs", [8, 2, 512], F32, at=after("ktok"))
        prob4 = place("prob4", [P, 4, 384], F32, at=after("kqs"))
        probT4 = place("probT4", [P, 4, 384], F32, at=after("prob4"))
        decay4 = place("decay4", [P, 4, 384], F32, at=after("probT4"))
        vtok = place("vtok", [P, 2, 512], F32, at=after("decay4"))
        vs8 = place("vs8", [8, 512], F32, at=after("vtok"))
        assert after("vs8") <= made["page"][0]
        rk2 = place("rk2", [P, 2, 2, T], F32, at=region)
        rq2 = place("rq2", [P, 2, 2, T], F32, at=after("rk2"))
        rv2 = place("rv2", [P, 2, 2, T], F32, at=after("rq2"))
        sg2 = place("sg2", [P, 2, 2, T], F32, at=after("rv2"))
        kdtok = place("kdtok", [P, 2, 2, 256], F32, at=after("sg2"))
        vtok2 = place("vtok2", [P, 2, 2, 256], F32, at=after("kdtok"))
        sT2 = place("sT2", [P, 2, 384], F32, at=after("vtok2"))
        oR = place("oR", [P, 2, 2, 256], F32, at=after("sT2"))
        sqR = place("sqR", [P, 2, 2, 256], F32, at=after("oR"))
        stR = place("stR", [P, 2, 512], F32, at=after("sqR"))
        vr8 = place("vr8", [8, 512], F32, at=after("stR"))
        assert after("vr8") <= made["page"][0]
        mix_hi = place("mix_hi", [P, DT, T], F32R, at=made["stateS"][0])
        mix_lo = place("mix_lo", [P, DT, T], F32R, at=after("mix_hi"))
        usum = place("usum", [P, 2, T], F32, at=after("mix_lo"))
        assert after("usum") <= made["cst"][0]
        uT = place("uT", [P, DT, T], F32, at=region)
        x1_hi = place("x1_hi", [P, DT, T], F32R, at=made["orT_hi"][0])
        x1_lo = place("x1_lo", [P, DT, T], F32R, at=after("x1_hi"))
        assert after("x1_lo") <= region
        scr = made["hT_hi"][0]
        lnsq = place("lnsq", [P, 2, 4, T], F32, at=scr)
        rstd = place("rstd", [P, T], F32, at=after("lnsq"))
        sgt = place("sgt", [P, 2, T], F32, at=after("rstd"))
        gact = place("gact", [P, 2, T], F32, at=after("sgt"))
        ytok = place("ytok", [P, 4, 512], F32, at=after("gact"))
        assert after("ytok") <= made["orT_hi"][0]
        g_hi = place("g_hi", [P, HF2, T], F32R, at=after("uT"))
        g_lo = place("g_lo", [P, HF2, T], F32R, at=after("g_hi"))
        assert after("g_lo") <= made["usum"][0]

        acc = [ctx.enter_context(nc.psum_tensor(f"acc{i}", [P, 2, 512], F32)) for i in range(2)]
        X = ctx.enter_context(nc.psum_tensor("X", [P, 4, 512], F32))

        q_rows = nc.dram_tensor("q_rows", [DEC, 1024], F32, kind="Internal").ap()
        v_rows = nc.dram_tensor("v_rows", [DEC, 1024], F32, kind="Internal").ap()

        def sem(name):
            return ctx.enter_context(nc.semaphore(name))

        raw_in = [sem(f"raw_in{i}") for i in range(RING)]
        y_stored = [sem(f"y_stored{i}") for i in range(4)]
        page_in = [sem(f"page_in{i}") for i in range(PAGES)]
        names = """hi_made lo_made multiplied act_step dve_step x_in cst_in parrows_in wff_in bf_in ptab_in
          p_in cst_par xn_made xT_ps h_made h_hi h_lo ff_ps ln_std lsg_abs lsg_ln logf_made lfn_made
          out_logf pT_ps p_hi p_made past_in decay_ps
          f_evac f_ktok_ps f_ktok_sb f_score_ps f_score_sb f_exp f_prob f_probT_ps f_probT_sb f_vtok_ps
          f_vtok_sb f_o_ps f_o_hi f_o_lo f_store_k f_store_v f_decay
          snew_ps snew_made bias_made
          r_evac r_rope r_ps1 r_kd_sb r_st_sb r_v_ps r_v_sb r_o_ps r_o_sb r_s_ps r_s_sb r_mean_ps r_cen
          r_sq r_var_ps r_std r_y r_hi r_lo r_store_s r_store_v
          q_in q_used page_used sc_made sc_ps s8_made e8_made p8_made p8_ps probT_made pv_ps of_made
          st_in vb_in st_scaled st_new st_ps or_made st_stored g_evac
          t_pb_ps t_of t_mean_ps t_cen t_sq t_var_ps t_std t_or t_hi t_lo
          mix_made mix_hi_made mix_lo_made u_made lnm_ps cen_made sq_made lnv_ps lnstd_made x1_made x1_hi_made x1_lo_made
          sg_made r_res g_act g_made g_hi_made g_lo_made y_made yT_ps y_tok acc0_free acc1_free pool_step sp_step""".split()
        S = {n: sem(n) for n in names}
        free = [S["acc0_free"], S["acc1_free"]]

        W = {k: a[k] for k in ("w_in", "w_ret_proj", "w_fox_proj", "w_out", "w1", "w3", "w2", "w_pg", "w_pe")}

        def piece(w, col, kt0, n_kt):
            def src(it):
                return w[kt0 * P:(kt0 + n_kt) * P, ds(col(it), NC)].rearrange("(t p) n -> p t n", p=P)
            return src

        def group(w, col, rhs, n_tiles, acc_i, kt_row0=0, ready=None):
            out = []
            for k in range(0, n_tiles, KT):
                n = min(KT, n_tiles - k)
                out.append(Chunk(piece(w, col, kt_row0 + k, n), rhs, k, n, acc_i, k == 0, k + n == n_tiles,
                                 ready and ready(k + n)))
            return out

        plan = {"chunks": 0, "groups": [0, 0]}
        RQ, RK, RV, RG, FQ, FK, FV, FF = (1024 * i for i in range(8))
        GR = FF + H_F
        GF = GR + D
        h = (hT_hi, hT_lo)
        w_in = W["w_in"]

        def col(start, per, off):
            return lambda it: it * per + (start + off)

        def heads(order, per):
            out = []
            for start in order:
                for i in range(per // NC):
                    out += group(w_in, col(start, per, i * NC), h, DT, i % 2)
            return out
        phF = Phase(plan, 2, heads([FK, FQ, FV], 512))
        phR = Phase(plan, 2, heads([RK, RQ, RV, RG], 512))
        phG = Phase(plan, 4, sum((group(w_in, col(g0, 512, i * NC), h, DT, n) for i in range(2) for n, g0 in enumerate((GR, GF))), []))
        phY = Phase(plan, 8, group(W["w_ret_proj"], col(0, NC, 0), (orT_hi, orT_lo), 8, 0)
                    + group(W["w_fox_proj"], col(0, NC, 0), (ofT_hi, ofT_lo), 8, 1))
        phO = Phase(plan, 4, sum((group(W["w_out"], col(0, 512, i * NC), (mix_hi, mix_lo), DT, i,
                                        ready=lambda k: ("mix_lo_made", k // 2)) for i in range(2)), []))
        phP = Phase(plan, 2, sum((group(W["w_pg"], col(0, 1024, i * NC), (x1_hi, x1_lo), DT, 0, ready=lambda k: ("x1_lo_made", k))
                                  + group(W["w_pe"], col(0, 1024, i * NC), (pT_hi, pT_lo), 2, 1) for i in range(4)), []))

        def down_chunks(half, col0):
            return sum((group(W["w2"], col(col0, 512, i * NC), (g_hi, g_lo), HF2, i, kt_row0=half * HF2,
                              ready=lambda k: ("g_lo_made", half * HF2 // 2 + k // 2)) for i in range(2)), [])
        ffn = []
        for half in range(2):
            up = Phase(plan, HF2 // 2, sum((group(W[w], col(half * HF2 * P, NC, 0), (x1_hi, x1_lo), DT, n) for n, w in enumerate(("w1", "w3"))), []))
            down = Phase(plan, 4 - half, down_chunks(half, 0))
            ffn.append((up, down))
        phLast = Phase(plan, 1, down_chunks(1, 3 * 512))

        block = ctx.enter_context(nc.Block())

        @block.sync
        def _(sp):
            sp.dma_start(xtok[:, 0:2, :], a["x_prompt"].rearrange("(t p) d -> p t d", p=P)).then_inc(S["x_in"], 16)
            sp.dma_start(xtok[0:DEC, 2, :], a["x_sample"]).then_inc(S["x_in"], 16)

            def load(ph, it, j):
                c, n = ph.chunks[j], ph.number(it, j)
                src = c.src(it)
                sp.wait_ge(S["lo_made"], n + 1)
                sp.sem_inc(S["sp_step"], 1)
                sp.dma_start(raw[:, j % RING, 0:c.n_kt, :], src).then_inc(raw_in[j % RING], 16)

            def stream(ph):
                with sp.Fori(0, ph.iters) as it:
                    for j in range(len(ph.chunks)):
                        load(ph, it, j)
            for ph in (phF, phR, phG, phY, phO, phP):
                stream(ph)
            for up, down in ffn:
                stream(up)
                stream(down)
            for j in range(len(phLast.chunks)):
                load(phLast, 0, j)

        def slot_uses(ph, it, j):
            n_body, c0 = len(ph.chunks) // RING, ph.chunk0 // RING
            return it * n_body + (c0 + j // RING + 1)

        def split_hi(act, ph, it, j):
            n, s, k = ph.number(it, j), j % RING, ph.n_kt(j)
            act.wait_ge(raw_in[s], slot_uses(ph, it, j) * 16)
            act.wait_ge(S["multiplied"], n + 1)
            nc.scalar.activation(whi[:, s, 0:k, :], raw[:, s, 0:k, :], ACT.Copy).then_inc(S["hi_made"], 1)

        def split_lo(dve, ph, it, j):
            n, s, k = ph.number(it, j), j % RING, ph.n_kt(j)
            dve.wait_ge(S["hi_made"], n + 1)
            nc.vector.tensor_tensor(wlo[:, s, 0:k, :], raw[:, s, 0:k, :], whi[:, s, 0:k, :].bitcast(F32),
                                    ALU.subtract).then_inc(S["lo_made"], 1)

        def group_done(eng, ph, it, j):
            eng.wait_ge(S["multiplied"], ph.number(it, j) + (RING + 1))

        def acc2(i):
            return acc[i][:, :, 0:T]

        @block.tensor
        def _(pe):
            mm, tr = nc.tensor.matmul, nc.tensor.transpose
            pe.wait_ge(S["cst_in"], 16)
            pe.wait_ge(S["parrows_in"], 16 * 7)
            tr(X[:, 0, 0:104], prow[0:104, :], ident[0:104, 0:104]).then_inc(S["cst_par"], 1)
            pe.wait_ge(S["xn_made"], 3)
            for k in range(DT):
                b = k % 4
                if k == 0:
                    pe.wait_ge(S["cst_par"], 2)
                if k >= 4:
                    pe.wait_ge(S["h_made"], k - 3)
                for t in range(2):
                    tr(X[:, b, t * P:(t + 1) * P], xtok[:, t, k * P:(k + 1) * P], ident)
                tr(X[:, b, SEQ:T], xtok[0:DEC, 2, k * P:(k + 1) * P], ident[0:DEC, 0:DEC]).then_inc(S["xT_ps"], 1)
            pe.wait_ge(S["wff_in"], 16)
            pe.wait_ge(S["h_made"], DT)
            for t, (lo, n) in enumerate(((0, P), (P, P), (SEQ, DEC))):
                for k in range(DT):
                    last = mm(X[0:n, 0, t * 8:t * 8 + 8], h32[:, k, lo:lo + n], wff[:, k, :], start=k == 0, stop=k == DT - 1)
            last.then_inc(S["ff_ps"], 1)
            pe.wait_ge(S["p_in"], 32)
            for k in range(2):
                for t in range(2):
                    tr(X[:, 1 + k, t * P:(t + 1) * P], ptok[:, t, k * P:(k + 1) * P], ident)
                last = tr(X[:, 1 + k, SEQ:T], ptok[0:DEC, 2, k * P:(k + 1) * P], ident[0:DEC, 0:DEC])
            last.then_inc(S["pT_ps"], 1)
            pe.wait_ge(S["past_in"], 16 * DEC * NPG)
            L4 = Lc[:, :, :].rearrange("s (b p) h -> s b (p h)", b=DEC)
            D4 = X[:, 3, :].rearrange("s (b m) -> s b m", b=DEC)
            mm(D4, const("gt"), L4, start=True, stop=False)
            for s in range(1, NPG):
                last = mm(D4[:, :, 0:(NPG - s) * H_F], const("ones"), L4[:, :, s * H_F:NPG * H_F], start=False, stop=s == NPG - 1)
            last.then_inc(S["decay_ps"], 1)
            pe.wait_ge(S["logf_made"], 2)
            tr(X[0:H_F, 0, 64:64 + DEC], logfS[:, :], ident[0:8, 0:8]).then_inc(S["lfn_made"], 1)
            pe.wait_ge(S["h_lo"], DT)
            pe.wait_ge(S["p_made"], 1)
            pe.wait_ge(S["lfn_made"], 2)

            def multiply(ph, it, j):
                c, n, s = ph.chunks[j], ph.number(it, j), j % RING
                xh, xl = c.rhs
                if c.first:
                    pe.wait_ge(free[c.acc], ph.group(it, j) + 1)
                if c.ready:
                    pe.wait_ge(S[c.ready[0]], c.ready[1])
                pe.wait_ge(S["hi_made"], n + 1)
                for t in range(c.n_kt):
                    for m in range(2):
                        w = whi[:, s, t, m * P:(m + 1) * P]
                        mm(acc[c.acc][:, m, 0:T], w, xh[:, c.kt0 + t, :], start=c.first and t == 0, stop=False)
                        mm(acc[c.acc][:, m, 0:T], w, xl[:, c.kt0 + t, :], start=False, stop=False)
                pe.wait_ge(S["lo_made"], n + (RING + 1))
                for t in range(c.n_kt):
                    for m in range(2):
                        last = mm(acc[c.acc][:, m, 0:T], wlo[:, s, t, m * P:(m + 1) * P], xh[:, c.kt0 + t, :],
                                  start=False, stop=c.last and t == c.n_kt - 1)
                last.then_inc(S["multiplied"], 1)

            def fox_key_rows(it):
                pe.wait_ge(S["f_evac"], it * 6 + 4)
                for t in range(2):
                    for i in range(4):
                        tr(X[:, t, i * P:(i + 1) * P], kT4[:, i, t * P:(t + 1) * P], ident)
                for n, x in enumerate((kT4, qT4)):
                    for i in range(4):
                        last = tr(X[0:DEC, 2 + n, i * P:(i + 1) * P], x[:, i, SEQ:T], ident)
                last.then_inc(S["f_ktok_ps"], 1)

            def fox_scores(it):
                pe.wait_ge(S["f_ktok_sb"], it * 2 + 2)
                pe.wait_ge(S["f_decay"], it + 1)
                for i in range(4):
                    b = X[:, i, :]
                    mm(b[:, 0:P], qT4[:, i, 0:P], kT4[:, i, 0:P], start=True, stop=False)
                    mm(b[:, 0:P], const("le"), decay4[:, i, 0:P], start=False, stop=True)
                    mm(b[:, P:3 * P], qT4[:, i, P:SEQ], kT4[:, i, 0:SEQ], start=True, stop=False)
                    mm(b[:, P:3 * P], const("le"), decay4[:, i, P:3 * P], start=False, stop=False)
                    last = mm(b[:, P:2 * P], const("ones"), decay4[:, i, 0:P], start=False, stop=True)
                last.then_inc(S["f_score_ps"], 1)

            def fox_prob_T(it):
                pe.wait_ge(S["f_prob"], it + 1)
                for i in range(4):
                    for n in range(3):
                        last = tr(X[:, i, n * P:(n + 1) * P], prob4[:, i, n * P:(n + 1) * P], ident)
                last.then_inc(S["f_probT_ps"], 1)

            def fox_value_rows(it):
                pe.wait_ge(S["f_probT_sb"], it + 1)
                pe.wait_ge(S["f_evac"], it * 6 + 6)
                for t in range(2):
                    for i in range(4):
                        tr(X[:, t, i * P:(i + 1) * P], vT4[:, i, t * P:(t + 1) * P], ident)
                for i in range(4):
                    last = tr(X[0:DEC, 2, i * P:(i + 1) * P], vT4[:, i, SEQ:T], ident)
                last.then_inc(S["f_vtok_ps"], 1)

            def fox_out(it):
                pe.wait_ge(S["f_vtok_sb"], it * 2 + 2)
                for i in range(4):
                    o = X[:, 2 + i // 2, (i % 2) * SEQ:(i % 2 + 1) * SEQ]
                    mm(o, vtok[:, 0, i * P:(i + 1) * P], probT4[:, i, 0:SEQ], start=True, stop=False)
                    last = mm(o[:, P:SEQ], vtok[:, 1, i * P:(i + 1) * P], probT4[:, i, SEQ:3 * P], start=False, stop=True)
                last.then_inc(S["f_o_ps"], 1)

            with pe.Fori(0, phF.iters) as it:
                for j in range(len(phF.chunks)):
                    multiply(phF, it, j)
                    if j == 16:
                        fox_key_rows(it)
                    if j == 17:
                        fox_scores(it)
                    if j == 21:
                        fox_prob_T(it)
                fox_value_rows(it)
                fox_out(it)

            pe.wait_ge(S["snew_made"], 1)
            for b in range(DEC):
                last = mm(X[0:H_F, 0, b:b + 1], prodS[:, b, :], const("ones")[:, 0:1], start=True, stop=True)
            last.then_inc(S["snew_ps"], 1)

            def past_scores_T(w):
                pe.wait_ge(S["sc_made"], w + 1)
                for p in range(NPG):
                    last = tr(X[0:H_F, 1 + p // 4, (p % 4) * P:(p % 4 + 1) * P], scd[:, p, :], ident)
                last.then_inc(S["sc_ps"], 1)

            def past_probs_T(w):
                pe.wait_ge(S["of_made"], w)
                pe.wait_ge(S["p8_made"], w + 1)
                for p in range(NPG):
                    last = mm(X[:, 0, p * 8:p * 8 + 8], s8[:, p * P:(p + 1) * P], ident[0:8, 0:8], start=True, stop=True)
                last.then_inc(S["p8_ps"], 1)

            def past_values(w, p, batch):
                if p == 0:
                    pe.wait_ge(S["probT_made"], w + 1)
                s = (NPG + p) % PAGES
                pe.wait_ge(page_in[s], w * (16 * 2 * NPG // PAGES) + 16 * ((NPG + p) // PAGES + 1))
                for i in range(H_F):
                    last = mm(X[:, 0, 64 + i:65 + i], page[:, s, i * P:(i + 1) * P], probT[:, p, i:i + 1],
                              start=p == 0 and i == 0, stop=p == NPG - 1, skip_group_check=True)
                last.then_inc(S["pv_ps"], 1)

            def window(w, pos):
                if pos == 8:
                    past_scores_T(w)
                if pos == 10:
                    past_probs_T(w)
                if pos >= 12:
                    past_values(w, 2 * (pos - 12), w)
                    past_values(w, 2 * (pos - 12) + 1, w)

            def ret_scores(it):
                pe.wait_ge(S["of_made"], it * 2 + 1)
                pe.wait_ge(S["r_rope"], it * 4 + 4)
                for i in range(2):
                    for t in range(2):
                        for d in range(2):
                            tr(X[:, i, t * 256 + d * P:t * 256 + (d + 1) * P], rk2[:, i, d, t * P:(t + 1) * P], ident)
                for i in range(2):
                    for d in range(2):
                        mm(X[:, 2 + i, 0:SEQ], rk2[:, i, d, 0:P], rq2[:, i, d, 0:SEQ], start=d == 0, stop=d == 1)
                    for d in range(2):
                        last = mm(X[:, 2 + i, SEQ:3 * P], rk2[:, i, d, P:SEQ], rq2[:, i, d, P:SEQ], start=d == 0, stop=d == 1)
                last.then_inc(S["r_ps1"], 1)

            def ret_value_rows(it):
                pe.wait_ge(S["s8_made"], it * 2 + 2)
                pe.wait_ge(S["r_kd_sb"], it + 1)
                pe.wait_ge(S["r_st_sb"], it + 1)
                pe.wait_ge(S["r_evac"], it * 4 + 2)
                for i in range(2):
                    for t in range(2):
                        for d in range(2):
                            tr(X[:, 1 + i, t * 256 + d * P:t * 256 + (d + 1) * P], rv2[:, i, d, t * P:(t + 1) * P], ident)
                for i in range(2):
                    for d in range(2):
                        last = tr(X[0:DEC, 3, i * 256 + d * P:i * 256 + (d + 1) * P], rv2[:, i, d, SEQ:T], ident)
                last.then_inc(S["r_v_ps"], 1)

            def ret_out(it):
                pe.wait_ge(S["r_v_sb"], it * 2 + 2)
                for i in range(2):
                    for e in range(2):
                        o = X[:, 1 + i, e * SEQ:(e + 1) * SEQ]
                        mm(o, vtok2[:, i, 0, e * P:(e + 1) * P], sT2[:, i, 0:SEQ], start=True, stop=False)
                        last = mm(o[:, P:SEQ], vtok2[:, i, 1, e * P:(e + 1) * P], sT2[:, i, SEQ:3 * P], start=False, stop=True)
                last.then_inc(S["r_o_ps"], 1)

            def ret_state(it, i, bank):
                for d in range(2):
                    for t in range(2):
                        last = mm(X[:, bank, d * 256:(d + 1) * 256], kdtok[:, i, t, d * P:(d + 1) * P], vtok2[:, i, t, :],
                                  start=t == 0, stop=t == 1)
                last.then_inc(S["r_s_ps"], 1)

            def ret_sum(src, bank, signal):
                for i in range(2):
                    for e in range(2):
                        last = mm(X[:, bank, i * SEQ:(i + 1) * SEQ], const("ones"), src[:, i, e, :], start=e == 0, stop=e == 1)
                last.then_inc(S[signal], 1)

            with pe.Fori(0, phR.iters) as it:
                for j in range(len(phR.chunks)):
                    multiply(phR, it, j)
                    if j == 8:
                        pe.wait_ge(S["r_s_sb"], it * 2)
                        pe.wait_ge(S["r_std"], it)
                    if j == 24:
                        pe.wait_ge(S["r_kd_sb"], it + 1)
                        pe.wait_ge(S["r_st_sb"], it + 1)
                    window(it * 2 + j // 16, j % 16)
                    if j == 17:
                        ret_scores(it)
                    if j == 26:
                        ret_value_rows(it)
                    if j == 27:
                        ret_out(it)
                    if j == 28:
                        ret_state(it, 0, 3)
                        pe.wait_ge(S["r_o_sb"], it + 1)
                        ret_state(it, 1, 1)
                        ret_sum(oR, 2, "r_mean_ps")
                    if j == 30:
                        pe.wait_ge(S["r_sq"], it + 1)
                        ret_sum(sqR, 2, "r_var_ps")

            def state_out(it, n):
                k = it * 2 + n
                pe.wait_ge(S["st_new"], k + 1)
                pe.wait_ge(S["or_made"], k)
                for i in range(H_R):
                    for e in range(2):
                        for d in range(2):
                            last = mm(X[:, 3, i * 2 + e:i * 2 + e + 1], stateS[:, i, d, e * P:(e + 1) * P],
                                      rqS[:, i, d, ds(k, 1)], start=d == 0, stop=d == 1)
                last.then_inc(S["st_ps"], 1)

            pe.wait_ge(S["r_s_sb"], 4)
            pe.wait_ge(S["r_std"], 2)
            with pe.Fori(0, phG.iters) as it:
                for j in range(len(phG.chunks)):
                    multiply(phG, it, j)
                    window(it + 4, j)
                    if j == 4:
                        state_out(it, 0)
                    if j == 13:
                        state_out(it, 1)

            pe.wait_ge(S["t_pb_ps"], 1)
            mm(X[:, 1, 0:64], const("ones")[0:8, :], pdiag[:, :, :].rearrange("g h b -> g (h b)"), start=True, stop=True)\
                .then_inc(S["t_pb_ps"], 1)
            pe.wait_ge(S["or_made"], DEC)

            def sample_sum(src, bank, signal):
                for e in range(2):
                    last = mm(X[:, bank, 0:32], const("ones"), src[:, :, e, :], start=e == 0, stop=e == 1)
                last.then_inc(S[signal], 1)
            sample_sum(orS, 2, "t_mean_ps")
            pe.wait_ge(S["t_sq"], 1)
            sample_sum(small[:, 1, :].rearrange("p (h e b) -> p h e b", h=H_R, e=2), 3, "t_var_ps")
            pe.wait_ge(S["t_lo"], 2)
            pe.wait_ge(S["r_lo"], 2)
            pe.wait_ge(S["f_o_lo"], 2)

            def plain(ph):
                with pe.Fori(0, ph.iters) as it:
                    for j in range(len(ph.chunks)):
                        multiply(ph, it, j)
            plain(phY)
            plain(phO)

            def norm_sums(n):
                pe.wait_ge(S["u_made"], 4 * (n + 1))
                for m in range(2):
                    last = mm(X[:, 0, 0:T], const("ones"), usum[:, m, :], start=m == 0, stop=m == 1)
                last.then_inc(S["lnm_ps"], 1)
                for q in range(4):
                    pe.wait_ge(S["sq_made"], 4 * n + q + 1)
                    for k in range(4):
                        last = mm(X[:, 1, 0:T], const("ones"), lnsq[:, q % 2, k, :], start=q == 0 and k == 0, stop=q == 3 and k == 3)
                    last.then_inc(S["lnv_ps"], 1)
            norm_sums(0)
            plain(phP)
            for up, down in ffn:
                plain(up)
                plain(down)
            for j in range(len(phLast.chunks)):
                multiply(phLast, 0, j)
            norm_sums(1)
            for q in range(4):
                pe.wait_ge(S["y_made"], q + 1)
                for t, n in enumerate((P, P, DEC)):
                    k3 = q * 3 + t
                    if k3 >= 2:
                        pe.wait_ge(S["y_tok"], k3 - 1)
                    for k in range(4):
                        last = tr(X[0:n, 2 + k3 % 2, k * P:(k + 1) * P], uT[:, q * 4 + k, t * P:t * P + n], ident)
                    last.then_inc(S["yT_ps"], 1)

        @block.scalar
        def _(act):
            A = nc.scalar.activation
            link = Chain(act, S["act_step"])
            act.dma_start(cst[:, :], a["shape_constants"]).then_inc(S["cst_in"], 16)
            for n, name in enumerate(("ln_emb_g", "ln_emb_b", "ln1_g", "ln1_b", "ln2_g", "ln2_b")):
                act.dma_start(prow[n * 16:(n + 1) * 16, :], a[name].rearrange("(r c) -> r c", c=P)).then_inc(S["parrows_in"], 16)
            act.dma_start(prow[96:104, :], a["gn_g"].rearrange("(r c) -> r c", c=P)).then_inc(S["parrows_in"], 16)
            act.dma_start(wff[:, :, :], a["w_in"][:, FF:FF + H_F].rearrange("(t p) n -> p t n", p=P)).then_inc(S["wff_in"], 16)
            act.dma_start(bf[:, :], a["b_f"].rearrange("(o n) -> o n", o=1).partition_broadcast(P)).then_inc(S["bf_in"], 16)
            act.dma_start(ptok[:, 0:2, :], a["p_prompt"].rearrange("(t p) d -> p t d", p=P)).then_inc(S["p_in"], 16)
            act.dma_start(ptok[0:DEC, 2, :], a["p_sample"]).then_inc(S["p_in"], 16)
            act.wait_ge(S["cst_in"], 16)
            act.wait_ge(S["ln_std"], 3)
            eps_ln, eps_gn = const("eps")[:, 0:1], const("eps")[:, 1:2]
            for t, n in enumerate((P, P, DEC)):
                last = A(stat[0:n, 40 + t:41 + t], stat[0:n, 32 + 2 * t + 1:32 + 2 * t + 2], ACT.Sqrt, bias=eps_ln[0:n, :])
            last.then_inc(S["ln_std"], 1)
            for k in range(DT):
                act.wait_ge(S["h_made"], k + 1)
                A(hT_hi[:, k, :], h32[:, k, :], ACT.Copy).then_inc(S["h_hi"], 1)
                if k % 6 == 5 and k // 6 < 1:
                    split_hi(act, phF, 0, 0)
            for j in range(1, AHEAD):
                split_hi(act, phF, 0, j)
            act.wait_ge(S["lsg_abs"], 1)
            link.step(A(stat[:, 0:16], stat[:, 0:16], ACT.Exp, scale=-1.0))
            link.step(A(small[0:8, 3, 0:8], small[0:8, 3, 0:8], ACT.Exp, scale=-1.0))
            A(stat[:, 0:16], stat[:, 0:16], ACT.Ln, bias=1.0)
            A(small[0:8, 3, 0:8], small[0:8, 3, 0:8], ACT.Ln, bias=1.0).then_inc(S["lsg_ln"], 1)
            act.wait_ge(S["pT_ps"], 1)
            A(pT_hi[:, :, :], X[:, 1:3, 0:T], ACT.Copy).then_inc(S["p_hi"], 1)

            with act.Fori(0, phF.iters) as it:
                link.enter(it, 16)
                for j in range(len(phF.chunks)):
                    split_hi(act, phF, it, j + AHEAD)
                    if phF.chunks[j].last:
                        g = j // 4
                        dst, src_s, i0 = ((kT4, kS, 0), (kT4, kS, 2), (qT4, qS, 0), (qT4, qS, 2), (vT4, vS, 0), (vT4, vS, 2))[g]
                        group_done(act, phF, it, j)
                        if g == 0:
                            act.wait_ge(S["f_o_hi"], it)
                        ac = phF.chunks[j].acc
                        A(dst[:, i0:i0 + 2, :], acc2(ac), ACT.Copy, scale=QS if dst is qT4 else 1.0).then_inc(free[ac], 1)
                        act.wait_ge(free[ac], phF.group(it, j) + 2)
                        A(src_s[:, ds(it * 4 + i0, 2), :], dst[:, i0:i0 + 2, SEQ:T], ACT.Copy).then_inc(S["f_evac"], 1)
                    if j == 16:
                        act.wait_ge(S["f_ktok_ps"], it + 1)
                        act.wait_ge(S["f_store_k"], it * 48)
                        A(ktok[:, :, :], X[:, 0:2, :], ACT.Copy).then_inc(S["f_ktok_sb"], 1)
                        A(kqs[:, :, :], X[0:DEC, 2:4, :], ACT.Copy).then_inc(S["f_ktok_sb"], 1)
                    if j == 17:
                        act.wait_ge(S["f_score_sb"], it + 1)
                        for i in range(4):
                            A(prob4[:, i, 0:P], prob4[:, i, 0:P], ACT.Exp, bias=softs[:, i:i + 1], accum_out=softs[:, 8 + i:9 + i])
                            last = A(prob4[:, i, P:3 * P], prob4[:, i, P:3 * P], ACT.Exp, bias=softs[:, 4 + i:5 + i],
                                     accum_out=softs[:, 12 + i:13 + i])
                        last.then_inc(S["f_exp"], 1)
                    if j == 21:
                        act.wait_ge(S["f_probT_ps"], it + 1)
                        A(probT4[:, :, :], X[:, :, 0:3 * P], ACT.Copy).then_inc(S["f_probT_sb"], 1)
                act.wait_ge(S["f_vtok_ps"], it + 1)
                act.wait_ge(S["f_store_v"], it * 32)
                A(vtok[:, :, :], X[:, 0:2, :], ACT.Copy).then_inc(S["f_vtok_sb"], 1)
                A(vs8[:, :], X[0:DEC, 2, :], ACT.Copy).then_inc(S["f_vtok_sb"], 1)
                act.wait_ge(S["f_o_ps"], it + 1)
                A(ofT_hi[:, ds(it * 4, 4), 0:SEQ], X[:, 2:4, :].rearrange("p b (i t) -> p (b i) t", i=2), ACT.Copy)\
                    .then_inc(S["f_o_hi"], 1)
                link.leave(phF.iters)

            def window(w, pos):
                if pos == 9:
                    act.wait_ge(S["s8_made"], w + 1)
                    A(s8[:, 0:1025], s8[:, 0:1025], ACT.Exp, bias=softs[0:8, 20:21], accum_out=softs[0:8, 21:22])\
                        .then_inc(S["e8_made"], 1)

            act.wait_ge(S["f_store_k"], 96)
            act.wait_ge(S["f_store_v"], 64)
            act.wait_ge(S["f_o_lo"], 2)
            with act.Fori(0, phR.iters) as it:
                link.enter(it, 16)
                for j in range(len(phR.chunks)):
                    split_hi(act, phR, it, j + AHEAD)
                    window(it * 2 + j // 16, j % 16)
                    if phR.chunks[j].last and j >= 16:
                        g = j // 4 - 4
                        ac = phR.chunks[j].acc
                        group_done(act, phR, it, j)
                        if g < 2:
                            A(rv2[:, g, :, :], acc2(ac), ACT.Copy).then_inc(free[ac], 1)
                            act.wait_ge(free[ac], phR.group(it, j) + 2)
                            act.nop().then_inc(S["r_evac"], 1)
                        else:
                            act.wait_ge(S["r_y"], it)
                            A(sg2[:, g - 2, :, :], acc2(ac), ACT.Silu).then_inc(free[ac], 1)
                            act.wait_ge(free[ac], phR.group(it, j) + 2)
                            A(sgS[:, ds(it * 2 + (g - 2), 1), :, :].rearrange("p o d b -> p (o d) b"), sg2[:, g - 2, :, SEQ:T], ACT.Copy)\
                                .then_inc(S["r_evac"], 1)
                    if j == 17:
                        act.wait_ge(S["r_ps1"], it + 1)
                        A(rkS[:, ds(it * 2, 2), :, :].rearrange("p h d b -> p (h d) b"),
                          rk2[:, :, :, SEQ:T].rearrange("p h d b -> p (h d) b"), ACT.Copy, scale=1.0 / 16.0)
                        A(rqS[:, ds(it * 2, 2), :, :].rearrange("p h d b -> p (h d) b"),
                          rq2[:, :, :, SEQ:T].rearrange("p h d b -> p (h d) b"), ACT.Copy)
                        kd0 = where["kdec"][0]
                        for i in range(2):
                            for t in range(2):
                                last = A(kdtok[:, i, t, :], X[:, i, t * 256:(t + 1) * 256], ACT.Copy,
                                         scale=cst[:, ds(it * 4 + (kd0 + i * 2 + t), 1)])
                        last.then_inc(S["r_kd_sb"], 1)
                    if j == 26:
                        act.wait_ge(S["r_v_ps"], it + 1)
                        act.wait_ge(S["r_store_v"], it * 16)
                        A(vtok2[:, :, :, :].rearrange("p h t c -> p h (t c)"), X[:, 1:3, :], ACT.Copy).then_inc(S["r_v_sb"], 1)
                        A(vr8[:, :], X[0:DEC, 3, :], ACT.Copy).then_inc(S["r_v_sb"], 1)
                    if j == 27:
                        act.wait_ge(S["r_o_ps"], it + 1)
                        A(oR[:, :, :, :].rearrange("p h e t -> p h (e t)"), X[:, 1:3, :], ACT.Copy).then_inc(S["r_o_sb"], 1)
                    if j == 28:
                        for i, bank in ((0, 3), (1, 1)):
                            act.wait_ge(S["r_s_ps"], it * 2 + i + 1)
                            if i == 0:
                                act.wait_ge(S["r_store_s"], it * 16)
                            A(stR[:, i, :], X[:, bank, :], ACT.Copy).then_inc(S["r_s_sb"], 1)
                    if j == 29:
                        act.wait_ge(S["r_cen"], it + 1)
                        A(sqR[:, :, :, :].rearrange("p h e t -> p (h e t)"), oR[:, :, :, :].rearrange("p h e t -> p (h e t)"), ACT.Square)\
                            .then_inc(S["r_sq"], 1)
                    if j == 30:
                        act.wait_ge(S["r_var_ps"], it + 1)
                        link.step(A(sqR[:, :, 0, :], X[:, 2, :].rearrange("p (h t) -> p h t", h=2), ACT.Sqrt, bias=eps_gn, scale=1.0 / 256.0))
                        act.nop().then_inc(S["r_std"], 1)
                act.wait_ge(S["r_y"], it + 1)
                A(orT_hi[:, ds(it * 4, 4), 0:SEQ], oR[:, :, :, :].rearrange("p h e t -> p (h e) t"), ACT.Copy).then_inc(S["r_hi"], 1)
                link.leave(phR.iters)

            def state_scale(it, n):
                k = it * 2 + n
                act.wait_ge(S["st_in"], k * 16 + 16)
                for i in range(H_R):
                    last = A(stateS[:, i, :, :].rearrange("p d e -> p (d e)"), stateS[:, i, :, :].rearrange("p d e -> p (d e)"),
                             ACT.Copy, scale=gammas[i])
                last.then_inc(S["st_scaled"], 1)

            act.wait_ge(S["r_lo"], 2)
            act.wait_ge(S["r_store_s"], 32)
            act.wait_ge(S["r_store_v"], 32)
            with act.Fori(0, phG.iters) as it:
                for j in range(len(phG.chunks)):
                    split_hi(act, phG, it, j + AHEAD)
                    window(it + 4, j)
                    if phG.chunks[j].last:
                        g, ac = j // 4, phG.chunks[j].acc
                        group_done(act, phG, it, j)
                        A(gate[:, ds(it * 4 + g // 2 * 2, 2), ac, :], acc2(ac), ACT.Sigmoid).then_inc(free[ac], 1)
                    if j == 2:
                        state_scale(it, 0)
                    if j == 11:
                        state_scale(it, 1)

            act.wait_ge(S["t_of"], 1)
            A(ofT_hi[:, :, SEQ:T], small[:, 0, :].rearrange("p (h b) -> p h b", h=H_F), ACT.Copy).then_inc(S["t_hi"], 1)
            act.wait_ge(S["t_cen"], 1)
            A(small[:, 1, :], orS[:, :, :, :].rearrange("p h e b -> p (h e b)"), ACT.Square).then_inc(S["t_sq"], 1)
            act.wait_ge(S["t_var_ps"], 1)
            A(small[:, 2, 0:32], X[:, 3, 0:32], ACT.Sqrt, bias=eps_gn, scale=1.0 / 256.0).then_inc(S["t_std"], 1)
            act.wait_ge(S["t_or"], 1)
            A(orT_hi[:, :, SEQ:T], orS[:, :, :, :].rearrange("p h e b -> p (h e) b"), ACT.Copy).then_inc(S["t_hi"], 1)

            act.wait_ge(S["st_stored"], 16 * DEC)
            with act.Fori(0, phY.iters) as it:
                for j in range(len(phY.chunks)):
                    split_hi(act, phY, it, j + AHEAD)
                act.wait_ge(S["mix_made"], it + 1)
                A(mix_hi[:, ds(it * 2, 2), :], gate[:, ds(it * 2, 2), 0, :], ACT.Copy).then_inc(S["mix_hi_made"], 1)
            with act.Fori(0, phO.iters) as it:
                for j in range(len(phO.chunks)):
                    split_hi(act, phO, it, j + AHEAD)

            def norm(n):
                for q in range(4):
                    act.wait_ge(S["cen_made"], 4 * n + q + 1)
                    if q >= 2:
                        act.wait_ge(S["lnv_ps"], 4 * n + q - 1)
                    A(lnsq[:, q % 2, :, :], uT[:, q * 4:q * 4 + 4, :], ACT.Square).then_inc(S["sq_made"], 1)
                act.wait_ge(S["lnv_ps"], 4 * n + 4)
                A(rstd[:, :], X[:, 1, 0:T], ACT.Sqrt, bias=eps_ln, scale=1.0 / D).then_inc(S["lnstd_made"], 1)
            norm(0)
            for k in range(DT):
                act.wait_ge(S["x1_made"], k + 1)
                A(x1_hi[:, k, :], uT[:, k, :], ACT.Copy).then_inc(S["x1_hi_made"], 1)

            with act.Fori(0, phP.iters) as it:
                for j in range(len(phP.chunks)):
                    split_hi(act, phP, it, j + AHEAD)
                    if j % 5 == 3:
                        group_done(act, phP, it, j)
                        act.wait_ge(S["r_res"], it * 4 + j // 5)
                        A(sgt[:, :, :], acc2(0), ACT.Sigmoid).then_inc(free[0], 1)
            for half, (up, down) in enumerate(ffn):
                with act.Fori(0, up.iters) as it:
                    for j in range(len(up.chunks)):
                        split_hi(act, up, it, j + AHEAD)
                        if j == 3:
                            group_done(act, up, it, j)
                            act.wait_ge(S["g_lo_made"], it + half * HF2 // 2)
                            A(gact[:, :, :], acc2(0), ACT.Silu).then_inc(free[0], 1)
                        if j == 7:
                            act.wait_ge(S["g_made"], it + (half * HF2 // 2 + 1))
                            A(g_hi[:, ds(it * 2, 2), :], gact[:, :, :], ACT.Copy).then_inc(S["g_hi_made"], 1)
                with act.Fori(0, down.iters) as it:
                    for j in range(len(down.chunks)):
                        split_hi(act, down, it, j + AHEAD)
            for j in range(AHEAD, len(phLast.chunks)):
                split_hi(act, phLast, 0, j)
            norm(1)

        @block.vector
        def _(dve):
            V = nc.vector
            link = Chain(dve, S["dve_step"])
            dve.sem_inc(S["lo_made"], RING)
            dve.sem_inc(S["multiplied"], RING)
            dve.sem_inc(free[0], 1)
            dve.sem_inc(free[1], 1)
            dve.wait_ge(S["x_in"], 32)
            for t, n in enumerate((P, P, DEC)):
                for q in range(4):
                    ins = V.bn_stats(small[0:n, t, q * 6:q * 6 + 6], xtok[0:n, t, q * 512:(q + 1) * 512])
                link.step(ins)
                V.bn_aggr(stat[0:n, 32 + 2 * t:34 + 2 * t], small[0:n, t, 0:24]).then_inc(S["ln_std"], 1)
            dve.wait_ge(S["ln_std"], 4)
            for t, n in enumerate((P, P, DEC)):
                ins = V.reciprocal(stat[0:n, 44 + t:45 + t], stat[0:n, 40 + t:41 + t])
            link.step(ins)
            for t, n in enumerate((P, P, DEC)):
                V.tensor_scalar(xtok[0:n, t, :], xtok[0:n, t, :], stat[0:n, 32 + 2 * t:33 + 2 * t], stat[0:n, 44 + t:45 + t],
                                ALU.subtract, ALU.mult).then_inc(S["xn_made"], 1)
            dve.wait_ge(S["cst_par"], 1)
            V.tensor_copy(par[:, :], X[:, 0, 0:104]).then_inc(S["cst_par"], 1)
            dve.wait_ge(S["cst_par"], 2)
            for k in range(DT):
                dve.wait_ge(S["xT_ps"], k + 1)
                V.tensor_scalar(h32[:, k, :], X[:, k % 4, 0:T], par[:, k:k + 1], par[:, 16 + k:17 + k], ALU.mult, ALU.add)\
                    .then_inc(S["h_made"], 1)
                if k >= 1:
                    dve.wait_ge(S["h_hi"], k)
                    V.tensor_tensor(hT_lo[:, k - 1, :], h32[:, k - 1, :], hT_hi[:, k - 1, :].bitcast(F32), ALU.subtract)\
                        .then_inc(S["h_lo"], 1)
            dve.wait_ge(S["h_hi"], DT)
            V.tensor_tensor(hT_lo[:, DT - 1, :], h32[:, DT - 1, :], hT_hi[:, DT - 1, :].bitcast(F32), ALU.subtract)\
                .then_inc(S["h_lo"], 1)
            for j in range(AHEAD):
                split_lo(dve, phF, 0, j)
            dve.wait_ge(S["ff_ps"], 1)
            dve.wait_ge(S["bf_in"], 16)
            zt, zs = stat[:, 16:32], small[0:8, 3, 8:16]
            V.tensor_tensor(zt.rearrange("p (t h) -> p t h", t=2), X[:, 0, 0:16].rearrange("p (t h) -> p t h", t=2),
                            bf[:, :].unsqueeze(1).broadcast_to([P, 2, H_F]), ALU.add)
            link.step(V.tensor_tensor(zs, X[0:8, 0, 16:24], bf[0:8, :], ALU.add))
            V.tensor_scalar(stat[:, 0:16], zt, -1.0, None, ALU.mult)
            link.step(V.tensor_scalar(small[0:8, 3, 0:8], zs, -1.0, None, ALU.mult))
            V.tensor_tensor(stat[:, 0:16], stat[:, 0:16], zt, ALU.max)
            link.step(V.tensor_tensor(small[0:8, 3, 0:8], small[0:8, 3, 0:8], zs, ALU.max))
            V.tensor_scalar(zt, zt, 0.0, None, ALU.min)
            V.tensor_scalar(zs, zs, 0.0, None, ALU.min).then_inc(S["lsg_abs"], 1)
            dve.wait_ge(S["lsg_ln"], 1)
            dve.wait_ge(S["lsg_abs"], 1)
            V.tensor_tensor(logf_tok[:, :, :].rearrange("p t h -> p (t h)"), zt, stat[:, 0:16], ALU.subtract).then_inc(S["logf_made"], 1)
            V.tensor_tensor(logfS[:, :], zs, small[0:8, 3, 0:8], ALU.subtract).then_inc(S["logf_made"], 1)
            dve.wait_ge(S["p_hi"], 1)
            V.tensor_tensor(pT_lo[:, :, :], X[:, 1:3, 0:T], pT_hi[:, :, :].bitcast(F32), ALU.subtract).then_inc(S["p_made"], 1)
            dve.wait_ge(S["decay_ps"], 1)
            V.tensor_copy(bias_past[:, :, :, :].rearrange("s b p h -> s (b p h)"), X[:, 3, :]).then_inc(S["bias_made"], 1)
            dve.wait_ge(S["lfn_made"], 1)
            V.tensor_copy(lfn8[:, :], X[0:8, 0, 64:72]).then_inc(S["lfn_made"], 1)
            dve.wait_ge(S["logf_made"], 2)
            dve.wait_ge(S["lfn_made"], 2)

            with dve.Fori(0, phF.iters) as it:
                link.enter(it, 24)
                for j in range(len(phF.chunks)):
                    split_lo(dve, phF, it, j + AHEAD)
                    if j == 8:
                        dve.wait_ge(S["f_o_hi"], it)
                        link.step(V.tensor_copy(lf4[:, :, :], logf_tok[:, :, ds(it * 4, 4)]))
                        V.tensor_tensor(decay4[:, :, 0:P], const("gt").unsqueeze(1).broadcast_to([P, 4, P]),
                                        lf4[:, 0, :].unsqueeze(2).broadcast_to([P, 4, P]), ALU.mult)
                        at = where["ones"][0]
                        V.tensor_tensor(decay4[:, :, P:3 * P], cst[:, at:at + 256].unsqueeze(1).broadcast_to([P, 4, 256]),
                                        lf4[:, 1, :].unsqueeze(2).broadcast_to([P, 4, 256]), ALU.mult).then_inc(S["f_decay"], 1)
                    if j == 17:
                        dve.wait_ge(S["f_score_ps"], it + 1)
                        link.step(V.tensor_tensor(prob4[:, :, :], X[:, :, 0:3 * P], const("mask").unsqueeze(1).broadcast_to([P, 4, 3 * P]), ALU.add))
                        V.tensor_reduce(softs[:, 0:4], prob4[:, :, 0:P], axis=AX.X, op=ALU.max)
                        link.step(V.tensor_reduce(softs[:, 4:8], prob4[:, :, P:3 * P], axis=AX.X, op=ALU.max))
                        V.tensor_scalar(softs[:, 0:8], softs[:, 0:8], -1.0, None, ALU.mult).then_inc(S["f_score_sb"], 1)
                    if j == 18:
                        dve.wait_ge(S["f_exp"], it + 1)
                        link.step(V.reciprocal(softs[:, 8:16], softs[:, 8:16]))
                        V.tensor_tensor(prob4[:, :, 0:P], prob4[:, :, 0:P], softs[:, 8:12].unsqueeze(2).broadcast_to([P, 4, P]), ALU.mult)
                        V.tensor_tensor(prob4[:, :, P:3 * P], prob4[:, :, P:3 * P], softs[:, 12:16].unsqueeze(2).broadcast_to([P, 4, 2 * P]), ALU.mult)\
                            .then_inc(S["f_prob"], 1)
                dve.wait_ge(S["f_o_hi"], it + 1)
                V.tensor_tensor(ofT_lo[:, ds(it * 4, 4), 0:SEQ], X[:, 2:4, :].rearrange("p b (i t) -> p (b i) t", i=2),
                                ofT_hi[:, ds(it * 4, 4), 0:SEQ].bitcast(F32), ALU.subtract).then_inc(S["f_o_lo"], 1)
                link.leave(phF.iters)

            dve.wait_ge(S["f_evac"], 12)
            V.tensor_tensor(prodS[:, :, :].rearrange("p b h -> p h b"), qS[:, :, :], kS[:, :, :], ALU.mult).then_inc(S["snew_made"], 1)
            dve.wait_ge(S["snew_ps"], 1)
            V.tensor_copy(snew8[:, :], X[0:8, 0, 0:DEC]).then_inc(S["snew_made"], 1)
            dve.wait_ge(S["snew_made"], 2)

            def window(w, pos):
                if pos < NPG:
                    s = pos % PAGES
                    if pos == 0:
                        dve.wait_ge(S["q_in"], w * 16 + 16)
                        dve.wait_ge(S["sc_made"], w)
                    dve.wait_ge(page_in[s], w * (16 * 2 * NPG // PAGES) + 16 * (pos // PAGES + 1))
                    for i in range(H_F):
                        last = V.tensor_tensor_reduce(out=pagesum[:, :], in0=page[:, s, i * P:(i + 1) * P], in1=qbc[:, i * P:(i + 1) * P],
                                                      scale=1.0, scalar=0.0, op0=ALU.mult, op1=ALU.add,
                                                      accum_out=sc8[:, pos, i:i + 1])
                        last.then_inc(S["page_used"], 1)
                        dve.wait_ge(S["page_used"], w * (NPG * H_F) + (pos * H_F + i + 1))
                if pos == 8:
                    dve.wait_ge(S["sc_ps"], w)
                    V.tensor_tensor(scd[:, :, :].rearrange("s p h -> s (p h)"), sc8[:, :, :].rearrange("s p h -> s (p h)"),
                                    bias_past[:, ds(w, 1), :, :].rearrange("s o p h -> s (o p h)"), ALU.add).then_inc(S["sc_made"], 1)
                if pos == 9:
                    dve.wait_ge(S["sc_ps"], w + 1)
                    link.step(V.tensor_scalar(s8[:, 0:1024], X[0:8, 1:3, :].rearrange("h b c -> h (b c)"), lfn8[:, ds(w, 1)], None, ALU.add))
                    link.step(V.tensor_copy(s8[:, 1024:1025], snew8[:, ds(w, 1)]))
                    link.step(V.tensor_reduce(softs[0:8, 20:21], s8[:, 0:1025], axis=AX.X, op=ALU.max))
                    V.tensor_scalar(softs[0:8, 20:21], softs[0:8, 20:21], -1.0, None, ALU.mult).then_inc(S["s8_made"], 1)
                if pos == 10:
                    dve.wait_ge(S["e8_made"], w + 1)
                    link.step(V.reciprocal(softs[0:8, 21:22], softs[0:8, 21:22]))
                    V.tensor_scalar(s8[:, 0:1025], s8[:, 0:1025], softs[0:8, 21:22], None, ALU.mult).then_inc(S["p8_made"], 1)
                    dve.wait_ge(S["p8_made"], w + 1)
                    V.tensor_copy(pnew8[:, ds(w, 1)], s8[:, 1024:1025])
                if pos == 11:
                    dve.wait_ge(S["p8_ps"], w + 1)
                    V.tensor_copy(probT[:, :, :].rearrange("s p h -> s (p h)"), X[:, 0, 0:64]).then_inc(S["probT_made"], 1)
                if pos == 15:
                    dve.wait_ge(S["pv_ps"], w * NPG + NPG)
                    V.tensor_copy(ofS[:, :, ds(w, 1)].rearrange("p h o -> p (h o)"), X[:, 0, 64:72]).then_inc(S["of_made"], 1)

            def rope(ph, it, j, dst):
                ac = ph.chunks[j].acc
                group_done(dve, ph, it, j)
                z = acc2(ac)
                V.tensor_tensor(dst, z, const("cos").unsqueeze(1).broadcast_to([P, 2, T]), ALU.mult)
                V.tensor_tensor(sqR2[:, 0, :], z[:, 1, :], const("nsin"), ALU.mult)
                V.tensor_tensor(sqR2[:, 1, :], z[:, 0, :], const("psin"), ALU.mult).then_inc(free[ac], 1)
                dve.wait_ge(free[ac], ph.group(it, j) + 2)
                V.tensor_tensor(dst, dst, sqR2[:, :, :], ALU.add).then_inc(S["r_rope"], 1)
                dve.wait_ge(S["r_rope"], it * 4 + (j // 4 + 1))

            sqR2 = stR[:, :, :].rearrange("p a b -> p (a b)")[:, 0:2 * T].rearrange("p (a b) -> p a b", a=2)
            dm0 = where["dmask"][0]
            dve.wait_ge(S["f_store_k"], 96)
            dve.wait_ge(S["f_store_v"], 64)
            with dve.Fori(0, phR.iters) as it:
                link.enter(it, 32)
                for j in range(len(phR.chunks)):
                    split_lo(dve, phR, it, j + AHEAD)
                    if phR.chunks[j].last and j < 16:
                        g = j // 4
                        if g == 0:
                            dve.wait_ge(S["r_store_s"], it * 16)
                            dve.wait_ge(S["r_hi"], it)
                        rope(phR, it, j, (rk2, rk2, rq2, rq2)[g][:, g % 2, :, :])
                    window(it * 2 + j // 16, j % 16)
                    if j == 17:
                        dve.wait_ge(S["r_ps1"], it + 1)
                        dm = cst[:, ds(it * 512 + dm0, 512)].rearrange("p (h t) -> p h t", h=2)
                        V.tensor_tensor(sT2[:, :, 0:SEQ], X[:, 2:4, 0:SEQ], dm, ALU.mult)
                        V.tensor_tensor(sT2[:, :, SEQ:3 * P], X[:, 2:4, SEQ:3 * P], dm[:, :, 0:P], ALU.mult).then_inc(S["r_st_sb"], 1)
                    if j == 28:
                        dve.wait_ge(S["r_mean_ps"], it + 1)
                        dve.wait_ge(S["r_o_sb"], it + 1)
                        for e in range(2):
                            last = V.scalar_tensor_tensor(out=oR[:, :, e, :], in0=X[:, 2, :].rearrange("p (h t) -> p h t", h=2),
                                                          scalar=-1.0 / 256.0, in1=oR[:, :, e, :], op0=ALU.mult, op1=ALU.add)
                        last.then_inc(S["r_cen"], 1)
                    if j == 31:
                        dve.wait_ge(S["r_std"], it + 1)
                        link.step(V.reciprocal(sqR[:, :, 1, :], sqR[:, :, 0, :]))
                        link.step(V.tensor_tensor(oR[:, :, :, :], oR[:, :, :, :], sqR[:, :, 1:2, :].broadcast_to([P, 2, 2, SEQ]), ALU.mult))
                        dve.wait_ge(S["r_evac"], it * 4 + 4)
                        for i in range(2):
                            for e in range(2):
                                last = V.scalar_tensor_tensor(out=oR[:, i, e, :], in0=oR[:, i, e, :], scalar=par[:, ds(it * 4 + (96 + i * 2 + e), 1)],
                                                              in1=sg2[:, i, e, 0:SEQ], op0=ALU.mult, op1=ALU.mult)
                        last.then_inc(S["r_y"], 1)
                        dve.wait_ge(S["r_hi"], it + 1)
                        V.tensor_tensor(orT_lo[:, ds(it * 4, 4), 0:SEQ], oR[:, :, :, :].rearrange("p h e t -> p (h e) t"),
                                        orT_hi[:, ds(it * 4, 4), 0:SEQ].bitcast(F32), ALU.subtract).then_inc(S["r_lo"], 1)
                link.leave(phR.iters)

            def state_new(it, n):
                k = it * 2 + n
                dve.wait_ge(S["st_scaled"], k + 1)
                dve.wait_ge(S["vb_in"], k * 16 + 16)
                for i in range(H_R):
                    for d in range(2):
                        last = V.scalar_tensor_tensor(out=stateS[:, i, d, :], in0=vbc[:, i, :], scalar=rkS[:, i, d, ds(k, 1)],
                                                      in1=stateS[:, i, d, :], op0=ALU.mult, op1=ALU.add)
                last.then_inc(S["st_new"], 1)

            def state_read(it, n):
                k = it * 2 + n
                dve.wait_ge(S["st_ps"], k + 1)
                V.tensor_copy(orS[:, :, :, ds(k, 1)].rearrange("p h e o -> p (h e o)"), X[:, 3, 0:8]).then_inc(S["or_made"], 1)

            with dve.Fori(0, phG.iters) as it:
                link.enter(it, 16)
                for j in range(len(phG.chunks)):
                    split_lo(dve, phG, it, j + AHEAD)
                    window(it + 4, j)
                    if j == 3:
                        state_new(it, 0)
                    if j == 5:
                        state_read(it, 0)
                    if j == 12:
                        state_new(it, 1)
                    if j == 14:
                        state_read(it, 1)
                link.leave(phG.iters)

            dve.wait_ge(S["of_made"], 8)
            V.tensor_tensor(pdiag[:, :, :], ident[0:8, 0:8].unsqueeze(2).broadcast_to([8, H_F, DEC]),
                            pnew8[:, :].unsqueeze(1).broadcast_to([8, H_F, DEC]), ALU.mult).then_inc(S["t_pb_ps"], 1)
            dve.wait_ge(S["t_pb_ps"], 2)
            of = small[:, 0, :]
            link.step(V.tensor_tensor(of, X[:, 1, 0:64], vS[:, :, :].rearrange("p h b -> p (h b)"), ALU.mult))
            V.tensor_tensor(of, of, ofS[:, :, :].rearrange("p h b -> p (h b)"), ALU.add).then_inc(S["t_of"], 1)
            dve.wait_ge(S["t_mean_ps"], 1)
            dve.wait_ge(S["or_made"], 8)
            for e in range(2):
                last = V.scalar_tensor_tensor(out=orS[:, :, e, :], in0=X[:, 2, 0:32].rearrange("p (h b) -> p h b", h=H_R), scalar=-1.0 / 256.0,
                                              in1=orS[:, :, e, :], op0=ALU.mult, op1=ALU.add)
            last.then_inc(S["t_cen"], 1)
            dve.wait_ge(S["t_hi"], 1)
            V.tensor_tensor(ofT_lo[:, :, SEQ:T], of.rearrange("p (h b) -> p h b", h=H_F), ofT_hi[:, :, SEQ:T].bitcast(F32), ALU.subtract)\
                .then_inc(S["t_lo"], 1)
            dve.wait_ge(S["t_std"], 1)
            link.step(V.reciprocal(small[:, 2, 32:64], small[:, 2, 0:32]))
            rec = small[:, 2, 32:64].rearrange("p (h b) -> p h b", h=H_R)
            for e in range(2):
                ins = V.tensor_tensor(orS[:, :, e, :], orS[:, :, e, :], rec, ALU.mult)
            link.step(ins)
            gn = par[:, 96:104].unsqueeze(2).broadcast_to([P, 8, DEC])
            o8 = orS[:, :, :, :].rearrange("p h e b -> p (h e) b")
            link.step(V.tensor_tensor(o8, o8, gn, ALU.mult))
            V.tensor_tensor(o8, o8, sgS[:, :, :, :].rearrange("p h e b -> p (h e) b"), ALU.mult).then_inc(S["t_or"], 1)
            dve.wait_ge(S["t_hi"], 2)
            V.tensor_tensor(orT_lo[:, :, SEQ:T], o8, orT_hi[:, :, SEQ:T].bitcast(F32), ALU.subtract).then_inc(S["t_lo"], 1)

            with dve.Fori(0, phY.iters) as it:
                link.enter(it, 4)
                for j in range(len(phY.chunks)):
                    split_lo(dve, phY, it, j + AHEAD)
                    if phY.chunks[j].last:
                        n = phY.chunks[j].acc
                        group_done(dve, phY, it, j)
                        g = gate[:, ds(it * 2, 2), n, :]
                        V.tensor_tensor(g, g, acc2(n), ALU.mult).then_inc(free[n], 1)
                for n in range(2):
                    dve.wait_ge(free[n], it + (phY.group0[n] + 2))
                V.tensor_tensor(gate[:, ds(it * 2, 2), 0, :], gate[:, ds(it * 2, 2), 0, :], gate[:, ds(it * 2, 2), 1, :], ALU.add)\
                    .then_inc(S["mix_made"], 1)
                dve.wait_ge(S["mix_hi_made"], it + 1)
                V.tensor_tensor(mix_lo[:, ds(it * 2, 2), :], gate[:, ds(it * 2, 2), 0, :], mix_hi[:, ds(it * 2, 2), :].bitcast(F32), ALU.subtract)\
                    .then_inc(S["mix_lo_made"], 1)
                link.leave(phY.iters)

            dve.wait_ge(S["mix_lo_made"], 8)
            link.step(V.memset(usum[:, :, :], 0.0))
            with dve.Fori(0, phO.iters) as it:
                link.enter(it, 8)
                for j in range(len(phO.chunks)):
                    split_lo(dve, phO, it, j + AHEAD)
                    if phO.chunks[j].last:
                        n = phO.chunks[j].acc
                        group_done(dve, phO, it, j)
                        k = it * 4 + n * 2
                        u = uT[:, ds(k, 2), :]
                        V.scalar_tensor_tensor(out=u, in0=hT_hi[:, ds(k, 2), :].bitcast(F32), scalar=ALPHA, in1=acc2(n), op0=ALU.mult, op1=ALU.add)\
                            .then_inc(free[n], 1)
                        dve.wait_ge(free[n], phO.group(it, j) + 2)
                        link.step(V.scalar_tensor_tensor(out=u, in0=hT_lo[:, ds(k, 2), :].bitcast(F32), scalar=ALPHA, in1=u, op0=ALU.mult, op1=ALU.add))
                        ins = V.tensor_tensor(usum[:, :, :], usum[:, :, :], u, ALU.add)
                        if n == 0:
                            link.step(ins)
                        else:
                            ins.then_inc(S["u_made"], 1)
                            dve.wait_ge(S["u_made"], it + 1)
                link.leave(phO.iters)

            def norm(n, g0):
                dve.wait_ge(S["lnm_ps"], n + 1)
                link.step(V.tensor_scalar(sgt[:, 0, :], X[:, 0, 0:T], 1.0 / D, None, ALU.mult))
                for q in range(4):
                    u = uT[:, q * 4:q * 4 + 4, :]
                    V.tensor_tensor(u, u, sgt[:, 0:1, :].broadcast_to([P, 4, T]), ALU.subtract).then_inc(S["cen_made"], 1)
                dve.wait_ge(S["lnstd_made"], n + 1)
                link.step(V.reciprocal(rstd[:, :], rstd[:, :]))
                dve.wait_ge(S["cen_made"], 4 * n + 4)
                dve.wait_ge(S["sq_made"], 4 * n + 4)
                for q in range(4):
                    u = uT[:, q * 4:q * 4 + 4, :]
                    link.step(V.tensor_tensor(u, u, rstd[:, :].unsqueeze(1).broadcast_to([P, 4, T]), ALU.mult))
                    for k in range(q * 4, q * 4 + 4):
                        ins = V.tensor_scalar(uT[:, k, :], uT[:, k, :], par[:, g0 + k:g0 + k + 1], par[:, g0 + 16 + k:g0 + 17 + k], ALU.mult, ALU.add)
                        if n == 0:
                            ins.then_inc(S["x1_made"], 1)
                    if n == 1:
                        ins.then_inc(S["y_made"], 1)
                    if n == 0:
                        for k in range(q * 4, q * 4 + 4):
                            dve.wait_ge(S["x1_hi_made"], k + 1)
                            V.tensor_tensor(x1_lo[:, k, :], uT[:, k, :], x1_hi[:, k, :].bitcast(F32), ALU.subtract).then_inc(S["x1_lo_made"], 1)
            norm(0, 32)

            with dve.Fori(0, phP.iters) as it:
                link.enter(it, 8)
                for j in range(len(phP.chunks)):
                    split_lo(dve, phP, it, j + AHEAD)
                    if j % 5 == 4:
                        i = j // 5
                        dve.wait_ge(free[0], phP.group(it, j - 1) + 2)
                        group_done(dve, phP, it, j)
                        V.tensor_tensor(sgt[:, :, :], sgt[:, :, :], acc2(1), ALU.mult).then_inc(free[1], 1)
                        dve.wait_ge(free[1], phP.group(it, j) + 2)
                        u = uT[:, ds(it * 8 + i * 2, 2), :]
                        V.scalar_tensor_tensor(out=u, in0=u, scalar=ALPHA, in1=sgt[:, :, :], op0=ALU.mult, op1=ALU.add).then_inc(S["r_res"], 1)
                link.leave(phP.iters)

            def down_step(ph, it, j, last_half):
                n = ph.chunks[j].acc
                group_done(dve, ph, it, j)
                u = uT[:, ds(it * 4 + n * 2, 2), :]
                V.tensor_tensor(u, u, acc2(n), ALU.add).then_inc(free[n], 1)
                if last_half:
                    dve.wait_ge(free[n], ph.group(it, j) + 2)
                    ins = V.tensor_tensor(usum[:, :, :], usum[:, :, :], u, ALU.add)
                    if n == 0:
                        link.step(ins)
                    else:
                        ins.then_inc(S["u_made"], 1)
                        dve.wait_ge(S["u_made"], it + 5)

            dve.wait_ge(S["r_res"], 8)
            link.step(V.memset(usum[:, :, :], 0.0))
            for half, (up, down) in enumerate(ffn):
                with dve.Fori(0, up.iters) as it:
                    for j in range(len(up.chunks)):
                        split_lo(dve, up, it, j + AHEAD)
                        if j == 7:
                            n_g = it + half * HF2 // 2
                            dve.wait_ge(free[0], up.group(it, 3) + 2)
                            group_done(dve, up, it, j)
                            V.tensor_tensor(gact[:, :, :], gact[:, :, :], acc2(1), ALU.mult).then_inc(free[1], 1)
                            dve.wait_ge(free[1], up.group(it, j) + 2)
                            dve.sem_inc(S["g_made"], 1)
                            dve.wait_ge(S["g_hi_made"], n_g + 1)
                            V.tensor_tensor(g_lo[:, ds(it * 2, 2), :], gact[:, :, :], g_hi[:, ds(it * 2, 2), :].bitcast(F32), ALU.subtract)\
                                .then_inc(S["g_lo_made"], 1)
                with dve.Fori(0, down.iters) as it:
                    link.enter(it, 4)
                    for j in range(len(down.chunks)):
                        split_lo(dve, down, it, j + AHEAD)
                        if down.chunks[j].last:
                            down_step(down, it, j, half == 1)
                    link.leave(down.iters)
            for j in range(len(phLast.chunks)):
                if j + AHEAD < len(phLast.chunks):
                    split_lo(dve, phLast, 0, j + AHEAD)
                if phLast.chunks[j].last:
                    n = phLast.chunks[j].acc
                    group_done(dve, phLast, 0, j)
                    u = uT[:, 12 + n * 2:14 + n * 2, :]
                    V.tensor_tensor(u, u, acc2(n), ALU.add).then_inc(free[n], 1)
                    dve.wait_ge(free[n], phLast.group(0, j) + 2)
                    ins = V.tensor_tensor(usum[:, :, :], usum[:, :, :], u, ALU.add)
                    if n == 0:
                        link.step(ins)
                    else:
                        ins.then_inc(S["u_made"], 1)
            norm(1, 64)
            for k3 in range(12):
                n = (P, P, DEC)[k3 % 3]
                dve.wait_ge(S["yT_ps"], k3 + 1)
                if k3 >= 4:
                    dve.wait_ge(y_stored[k3 % 4], 16 * (k3 // 4))
                V.tensor_copy(ytok[0:n, k3 % 4, :], X[0:n, 2 + k3 % 2, :]).then_inc(S["y_tok"], 1)

        @block.gpsimd
        def _(pool):
            pool.dma_start(ptab[:, :], a["page_table"]).then_inc(S["ptab_in"], 16)
            pool.wait_ge(S["ptab_in"], 16)
            with pool.Fori(0, DEC * NPG) as i:
                number = pool.value_load(ptab[0:1, ds(i, 1)], min_val=0, max_val=NPOOL - 1)
                pool.dma_start(Lc[:, ds(i, 1), :].rearrange("s o h -> s (o h)"), a["cache_logf"][ds(number, 1)].rearrange("o s h -> s (o h)"))\
                    .then_inc(S["past_in"], 16)
            pool.wait_ge(S["logf_made"], 2)
            pool.dma_start(a["fox_logf_prompt"].rearrange("(t p) h -> p t h", p=P), logf_tok[:, :, :]).then_inc(S["out_logf"], 16)
            pool.dma_start(a["fox_logf_sample"], logfS[:, :]).then_inc(S["out_logf"], 16)
            with pool.Fori(0, phF.iters) as it:
                cols = ds(it * 512, 512)
                pool.wait_ge(S["f_ktok_sb"], it * 2 + 2)
                pool.sem_inc(S["pool_step"], 1)
                pool.dma_start(a["fox_k_prompt"].rearrange("(t p) c -> p t c", p=P)[:, :, cols], ktok[:, :, :]).then_inc(S["f_store_k"], 16)
                pool.dma_start(a["fox_k_sample"][:, cols], kqs[:, 0, :]).then_inc(S["f_store_k"], 16)
                pool.dma_start(q_rows[:, cols], kqs[:, 1, :]).then_inc(S["f_store_k"], 16)
                pool.wait_ge(S["f_vtok_sb"], it * 2 + 2)
                pool.sem_inc(S["pool_step"], 1)
                pool.dma_start(a["fox_v_prompt"].rearrange("(t p) c -> p t c", p=P)[:, :, cols], vtok[:, :, :]).then_inc(S["f_store_v"], 16)
                pool.dma_start(a["fox_v_sample"][:, cols], vs8[:, :]).then_inc(S["f_store_v"], 16)
            pool.wait_ge(S["f_store_k"], 96)

            def load_page(w, n):
                p, s = n % NPG, n % PAGES
                cache = a["cache_k"] if n < NPG else a["cache_v"]
                if n < PAGES:
                    pool.wait_ge(S["pv_ps"], w * NPG)
                elif n < NPG + PAGES:
                    pool.wait_ge(S["page_used"], w * (NPG * H_F) + (n - PAGES + 1) * H_F)
                else:
                    pool.wait_ge(S["pv_ps"], w * NPG + (n - NPG - PAGES + 1))
                pool.sem_inc(S["pool_step"], 1)
                number = pool.value_load(ptab[0:1, ds(w * NPG + p, 1)], min_val=0, max_val=NPOOL - 1)
                pool.dma_start(page[:, s, :], cache[ds(number, 1)].rearrange("o s c -> s (o c)")).then_inc(page_in[s], 16)

            def load_query(w):
                pool.wait_ge(S["page_used"], w * (NPG * H_F))
                pool.sem_inc(S["pool_step"], 1)
                pool.dma_start(qbc[:, :], q_rows[ds(w, 1), :].partition_broadcast(P)).then_inc(S["q_in"], 16)

            def load_window(w):
                load_query(w)
                for n in range(2 * NPG):
                    load_page(w, n)

            with pool.Fori(0, phR.iters) as it:
                load_window(it * 2)
                load_window(it * 2 + 1)
                cols = ds(it * 512, 512)
                pool.wait_ge(S["r_v_sb"], it * 2 + 2)
                pool.sem_inc(S["pool_step"], 1)
                pool.dma_start(v_rows[:, cols], vr8[:, :]).then_inc(S["r_store_v"], 16)
                pool.wait_ge(S["r_s_sb"], it * 2 + 2)
                pool.sem_inc(S["pool_step"], 1)
                pool.dma_start(a["ret_state_prompt"][ds(it * 2, 2)].rearrange("h (d p) e -> p (h d) e", p=P),
                               stR[:, :, :].rearrange("p h (d e) -> p (h d) e", d=2)).then_inc(S["r_store_s"], 16)
            pool.wait_ge(S["r_store_v"], 32)
            pool.wait_ge(S["r_store_s"], 32)
            pool.wait_ge(S["r_lo"], 2)

            def load_state(it, n):
                k = it * 2 + n
                pool.wait_ge(S["st_ps"], k)
                pool.wait_ge(S["st_stored"], k * 16)
                pool.sem_inc(S["pool_step"], 1)
                pool.dma_start(stateS[:, :, :, :].rearrange("p h d e -> p (h d) e"),
                               a["state_ret"][ds(k, 1)].rearrange("o h (d p) e -> p (o h d) e", p=P)).then_inc(S["st_in"], 16)
                pool.dma_start(vbc[:, :, :].rearrange("p h e -> p (h e)"), v_rows[ds(k, 1), :].partition_broadcast(P)).then_inc(S["vb_in"], 16)

            def store_state(it, n):
                k = it * 2 + n
                pool.wait_ge(S["st_new"], k + 1)
                pool.sem_inc(S["pool_step"], 1)
                pool.dma_start(a["ret_state_sample"][ds(k, 1)].rearrange("o h (d p) e -> p (o h d) e", p=P),
                               stateS[:, :, :, :].rearrange("p h d e -> p (h d) e")).then_inc(S["st_stored"], 16)

            with pool.Fori(0, phG.iters) as it:
                load_state(it, 0)
                load_query(it + 4)
                for n in range(2 * NPG):
                    load_page(it + 4, n)
                    if n == 7:
                        store_state(it, 0)
                    if n == 10:
                        load_state(it, 1)
                store_state(it, 1)

            for k3 in range(12):
                q, t = divmod(k3, 3)
                n = (P, P, DEC)[t]
                pool.wait_ge(S["y_tok"], k3 + 1)
                dst = a["y_sample"][:, q * 512:(q + 1) * 512] if t == 2 else a["y_prompt"][t * P:(t + 1) * P, q * 512:(q + 1) * 512]
                pool.dma_start(dst, ytok[0:n, k3 % 4, :]).then_inc(y_stored[k3 % 4], 16)
            pool.wait_ge(S["out_logf"], 32)
            pool.wait_ge(S["f_store_k"], 96)
            pool.wait_ge(S["f_store_v"], 64)
            pool.wait_ge(S["r_store_s"], 32)
            pool.wait_ge(S["r_store_v"], 32)
            pool.wait_ge(S["st_stored"], 16 * DEC)
            for i in range(4):
                pool.wait_ge(y_stored[i], 16 * 3)


SLAB_BASE = 16512


def kernel(**inputs):
    import concourse.bacc as _bacc
    from concourse.bass_utils import run_bass_kernel_spmd as _run

    x = {k: np.asarray(v) for k, v in inputs.items()}
    _, SEQ, D = x["x_prompt"].shape
    DEC, NPG = x["page_table"].shape
    NPOOL, PAGE = x["cache_k"].shape[1:3]
    H_F, D_F = x["cache_k"].shape[3:]
    _, _, H_R, DK, DV = x["state_ret"].shape
    dims = {"D": D, "SEQ": SEQ, "DEC": DEC, "NPG": NPG, "NPOOL": NPOOL, "H_R": H_R, "H_F": H_F, "D_FF": x["w1"].shape[2]}
    blob, where, gammas = shape_constants(SEQ, DEC, NPG * PAGE, H_R)
    shaped = {
        "x_prompt": (SEQ, D), "x_sample": (DEC, D), "state_ret": (DEC, H_R, DK, DV),
        "cache_k": (NPOOL, PAGE, H_F * D_F), "cache_v": (NPOOL, PAGE, H_F * D_F), "cache_logf": (NPOOL, PAGE, H_F),
        "page_table": (1, DEC * NPG), "p_prompt": (SEQ, x["p_prompt"].shape[-1]), "p_sample": (DEC, x["p_sample"].shape[-1]),
        "gn_g": (H_R * DV,),
    }
    nc = _bacc.Bacc("TRN2", target_bir_lowering=False, num_devices=1)
    arrays, aps = {}, {}
    for name, v in {**x, "shape_constants": blob}.items():
        if name in shaped:
            v = v.reshape(shaped[name])
        elif v.ndim == 3 or name in ("b_f", "ln1_g", "ln1_b", "ln2_g", "ln2_b"):
            v = v.reshape(v.shape[1:])
        arrays["in_" + name] = np.ascontiguousarray(v)
        aps[name] = nc.dram_tensor("in_" + name, v.shape, mybir.dt.from_np(v.dtype), kind="ExternalInput").ap()
    outs = {
        "y_prompt": ((SEQ, D), (1, SEQ, D)), "y_sample": ((DEC, D), (DEC, 1, D)),
        "ret_state_prompt": ((H_R, DK, DV), (1, 1, H_R, DK, DV)),
        "fox_k_prompt": ((SEQ, H_F * D_F), (1, 1, SEQ, H_F, D_F)), "fox_v_prompt": ((SEQ, H_F * D_F), (1, 1, SEQ, H_F, D_F)),
        "fox_logf_prompt": ((SEQ, H_F), (1, 1, SEQ, H_F)),
        "ret_state_sample": ((DEC, H_R, DK, DV), (1, DEC, H_R, DK, DV)),
        "fox_k_sample": ((DEC, H_F * D_F), (1, DEC, 1, H_F, D_F)), "fox_v_sample": ((DEC, H_F * D_F), (1, DEC, 1, H_F, D_F)),
        "fox_logf_sample": ((DEC, H_F), (1, DEC, 1, H_F)),
    }
    for name, (shape, _) in outs.items():
        aps[name] = nc.dram_tensor("out_" + name, shape, F32, kind="ExternalOutput").ap()
    layer_kernel(nc, aps, where, gammas, dims)
    r = _run(nc, [arrays], core_ids=[0])
    return tuple(r.results[0]["out_" + name].reshape(full) for name, (_, full) in outs.items())
```

```python
from contextlib import ExitStack

import numpy as np

import concourse.bass as bass
from concourse import mybir

F32 = mybir.dt.float32
F32R = mybir.dt.float32r
I32 = mybir.dt.int32
ALU = mybir.AluOpType
ACT = mybir.ActivationFunctionType
AX = mybir.AxisListType
ds = bass.ds

P = 128
RING = 4
AHEAD = 3
PAGES = 4
KT = 4
NC = 256
HEADS = 4
HALVES = (32, 64)
BIG = -1.0e30


CREDIT = {"lo_made": RING, "multiplied": RING, "acc0_free": 1, "acc1_free": 1, "page_used": HEADS,
          "of_made": 1, "or_made": 1, "sc_made": 1, "sc_ps": 1, "r_res": 1, "g_lo_made": 1, "pv_ps": 1, "st_ps": 1}

KEY_POS = (0, 2, 4, 6, 8, 9, 11, 13)
VALUE_POS = (5, 7, 9, 10, 11, 12, 13, 14)
KEYS, VALUES = [("key", p) for p in range(8)], [("value", p) for p in range(8)]
ORDER = {"first": KEYS, "last": VALUES,
         "middle": sorted(KEYS + VALUES, key=lambda e: (KEY_POS[e[1]] if e[0] == "key" else VALUE_POS[e[1]], e))}


def line(slot, m, c):
    it, base = slot
    return base * m + c if it is None else it * m + (base * m + c)


def page_of(sort, slot, entry):
    n = ORDER[sort].index(entry)
    return n % PAGES, (n // PAGES + 1 if sort == "first" else line(slot, 16 // PAGES, n // PAGES - 1))


def shape_constants(SEQ, DEC, PAST, H_R):
    half = 128
    f = np.float32
    inv = (f(10000.0) ** (-np.arange(half, dtype=f) / f(half))).astype(f)
    pos = np.concatenate([np.arange(SEQ), np.full(DEC, PAST)]).astype(f)
    ang = inv[:, None] * pos[None, :]
    i = np.arange(P)
    le = (i[:, None] <= i[None, :]).astype(f)
    gt = (i[:, None] > i[None, :]).astype(f)
    ones = np.ones((P, P), f)
    causal = np.where(i[None, :] <= i[:, None], 0.0, BIG).astype(f)
    log_g = np.log1p(-np.exp2(-5.0 - np.arange(H_R, dtype=np.float64)))
    scale = 1.0 / 16.0
    j, t = np.arange(P)[:, None], np.arange(SEQ)[None, :]
    dmask = [np.where(t >= j, np.exp(lg * (t - j)) * scale, 0.0) for lg in log_g]
    kdec = [np.exp(lg * (SEQ - 1 - (blk * P + i)))[:, None] * scale for lg in log_g for blk in range(SEQ // P)]
    parts = {
        "ident": np.eye(P), "eps": np.tile([[1e-5, 1e-6]], (P, 1)), "le": le, "ones": ones, "gt": gt,
        "mask": np.concatenate([causal, np.zeros((P, P)), causal], 1),
        "cos": np.cos(ang), "nsin": -np.sin(ang), "psin": np.sin(ang),
        "dmask": np.concatenate(dmask, 1), "kdec": np.concatenate(kdec, 1),
    }
    at, where = 0, {}
    for k, a in parts.items():
        where[k] = (at, a.shape[1])
        at += a.shape[1]
    return np.concatenate([np.asarray(a, f) for a in parts.values()], 1).astype(f), where, [float(np.exp(x)) for x in log_g]


class Chunk:

    def __init__(self, src, rhs, kt0, n_kt, acc, first, last, ready=None):
        self.src, self.rhs, self.kt0, self.n_kt = src, rhs, kt0, n_kt
        self.acc, self.first, self.last, self.ready = acc, first, last, ready


class Phase:

    def __init__(self, plan, iters, chunks):
        assert len(chunks) % RING == 0
        self.iters, self.chunks, self.chunk0 = iters, chunks, plan["chunks"]
        self.group0 = list(plan["groups"])
        self.per = [sum(c.first for c in chunks if c.acc == a) for a in (0, 1)]
        plan["chunks"] += iters * len(chunks)
        for a in (0, 1):
            plan["groups"][a] += iters * self.per[a]

    def number(self, it, j):
        return it * len(self.chunks) + (self.chunk0 + j)

    def group(self, it, j):
        acc = self.chunks[j].acc
        before = sum(c.first for c in self.chunks[:j + 1] if c.acc == acc) - 1
        return it * self.per[acc] + (self.group0[acc] + before)

    def n_kt(self, j):
        return self.chunks[j % len(self.chunks)].n_kt


class Chain:

    def __init__(self, eng, sem):
        self.eng, self.sem, self.base, self.n = eng, sem, 0, 0

    def step(self, ins):
        self.n += 1
        ins.then_inc(self.sem, 1)
        self.eng.wait_ge(self.sem, self.base + self.n)

    def enter(self, it, per):
        self.start, self.per = self.base + self.n, per
        self.base, self.n = it * per + self.start, 0

    def leave(self, iters):
        assert self.n <= self.per, self.n
        if self.per > self.n:
            self.eng.sem_inc(self.sem, self.per - self.n)
        self.base, self.n = self.start + iters * self.per, 0


def layer_kernel(nc, a, where, gammas, dims):
    D, SEQ, DEC, NPG, NPOOL, H_R, H_F, D_FF = (dims[k] for k in ("D", "SEQ", "DEC", "NPG", "NPOOL", "H_R", "H_F", "D_FF"))
    T = SEQ + DEC
    DT = D // P
    NB = SEQ // P
    HF2 = D_FF // P // 2
    ALPHA = 2.0 ** 0.25
    QS = float(P) ** -0.5
    assert DT == 16 and NB == 2 and DEC == 8 and NPG == 8 and H_F == 8 and H_R == 4 and HF2 == 22

    ctx = ExitStack()
    with ctx:
        slab_bytes = 212800
        slab = ctx.enter_context(nc.sbuf_tensor("slab", [P, slab_bytes // 4], F32))
        base = SLAB_BASE
        top = [0]
        made = {}

        def place(name, shape, dt, at=None):
            size = int(np.prod(shape[1:])) * 4
            if at is None:
                at, top[0] = top[0], (top[0] + size + 31) // 32 * 32
            assert at % 32 == 0 and at + size <= slab_bytes, (name, at, size)
            made[name] = (at, size)
            return nc.alloc_sbuf_tensor_at(name, shape, dt, offset=base + at)

        def after(name):
            return (made[name][0] + made[name][1] + 31) // 32 * 32

        raw = place("raw", [P, RING, KT, NC], F32)
        whi = place("whi", [P, RING, KT, NC], F32R)
        wlo = place("wlo", [P, RING, KT, NC], F32R)
        hT_hi = place("hT_hi", [P, DT, T], F32R)
        hT_lo = place("hT_lo", [P, DT, T], F32R)
        orT_hi = place("orT_hi", [P, 8, T], F32R)
        orT_lo = place("orT_lo", [P, 8, T], F32R)
        ofT_hi = place("ofT_hi", [P, 8, T], F32R)
        ofT_lo = place("ofT_lo", [P, 8, T], F32R)
        region = top[0]
        gate = place("gate", [P, DT, 2, T], F32)
        stateS = place("stateS", [P, H_R, 2, 256], F32)
        vbc = place("vbc", [P, H_R, 256], F32)
        page = place("page", [P, PAGES, 1024], F32)
        qbc = place("qbc", [P, 1024], F32)
        s8 = place("s8", [8, 1032], F32)
        n_const = sum(w for _, w in where.values())
        cst = place("cst", [P, n_const], F32)
        par = place("par", [P, 104], F32)
        pT_hi = place("pT_hi", [P, 2, T], F32R)
        pT_lo = place("pT_lo", [P, 2, T], F32R)
        bias_past = place("bias_past", [P, DEC, NPG, H_F], F32)
        sc8 = place("sc8", [P, NPG, H_F], F32)
        scd = place("scd", [P, NPG, H_F], F32)
        pagesum = place("pagesum", [P, HEADS, P], F32)
        probT = place("probT", [P, NPG, H_F], F32)
        qS = place("qS", [P, H_F, DEC], F32)
        kS = place("kS", [P, H_F, DEC], F32)
        vS = place("vS", [P, H_F, DEC], F32)
        ofS = place("ofS", [P, H_F, DEC], F32)
        rqS = place("rqS", [P, H_R, 2, DEC], F32)
        rkS = place("rkS", [P, H_R, 2, DEC], F32)
        sgS = place("sgS", [P, H_R, 2, DEC], F32)
        orS = place("orS", [P, H_R, 2, DEC], F32)
        prodS = place("prodS", [P, DEC, H_F], F32)
        ov8 = place("ov8", [72, 512], F32, at=made["s8"][0])
        or8 = place("or8", [72, 512], F32, at=after("ov8"))
        rk1 = place("rk1", [P, H_R, 2, 1], F32)
        logf_tok = place("logf_tok", [P, NB, H_F], F32)
        lf4 = place("lf4", [P, NB, 4], F32)
        logfS = place("logfS", [8, H_F], F32)
        lfn8 = place("lfn8", [8, DEC], F32)
        snew8 = place("snew8", [8, DEC], F32)
        pnew8 = place("pnew8", [8, DEC], F32)
        pdiag = place("pdiag", [8, H_F, DEC], F32)
        bf = place("bf", [P, H_F], F32)
        ptab = place("ptab", [1, DEC * NPG], I32)
        stat = place("stat", [P, 64], F32)
        small = place("small", [P, 4, 64], F32)
        softs = place("softs", [P, 24], F32)

        def const(name, rows=P):
            at, n = where[name]
            return cst[0:rows, at:at + n]
        ident = const("ident")
        xtok = place("xtok", [P, 3, D], F32, at=region)
        h32 = place("h32", [P, DT, T], F32, at=after("xtok"))
        wff = place("wff", [P, DT, H_F], F32, at=after("h32"))
        ptok = place("ptok", [P, 3, 256], F32, at=after("wff"))
        prow = place("prow", [104, P], F32, at=after("ptok"))
        Lc = place("Lc", [P, DEC * NPG, H_F], F32, at=made["page"][0])
        kT4 = place("kT4", [P, 4, T], F32, at=region)
        qT4 = place("qT4", [P, 4, T], F32, at=after("kT4"))
        vT4 = place("vT4", [P, 4, T], F32, at=after("qT4"))
        ktok = place("ktok", [P, 2, 512], F32, at=after("vT4"))
        kqs = place("kqs", [8, 2, 512], F32, at=after("ktok"))
        prob4 = place("prob4", [P, 4, 384], F32, at=after("kqs"))
        probT4 = place("probT4", [P, 4, 384], F32, at=after("prob4"))
        decay4 = place("decay4", [P, 4, 384], F32, at=after("probT4"))
        vtok = place("vtok", [P, 2, 512], F32, at=after("decay4"))
        vs8 = place("vs8", [8, 512], F32, at=after("vtok"))
        assert after("vs8") <= made["page"][0]
        rk2 = place("rk2", [P, 2, 2, T], F32, at=region)
        rq2 = place("rq2", [P, 2, 2, T], F32, at=after("rk2"))
        rv2 = place("rv2", [P, 2, 2, T], F32, at=after("rq2"))
        sg2 = place("sg2", [P, 2, 2, T], F32, at=after("rv2"))
        kdtok = place("kdtok", [P, 2, 2, 256], F32, at=after("sg2"))
        vtok2 = place("vtok2", [P, 2, 2, 256], F32, at=after("kdtok"))
        sT2 = place("sT2", [P, 2, 384], F32, at=after("vtok2"))
        oR = place("oR", [P, 2, 2, 256], F32, at=after("sT2"))
        sqR = place("sqR", [P, 2, 2, 256], F32, at=after("oR"))
        stR = place("stR", [P, 2, 512], F32, at=after("sqR"))
        vr8 = place("vr8", [8, 512], F32, at=after("stR"))
        assert after("vr8") <= made["page"][0]
        mix_hi = place("mix_hi", [P, DT, T], F32R, at=made["stateS"][0])
        mix_lo = place("mix_lo", [P, DT, T], F32R, at=after("mix_hi"))
        usum = place("usum", [P, 2, T], F32, at=after("mix_lo"))
        assert after("usum") <= made["cst"][0]
        uT = place("uT", [P, DT, T], F32, at=region)
        x1_hi = place("x1_hi", [P, DT, T], F32R, at=made["orT_hi"][0])
        x1_lo = place("x1_lo", [P, DT, T], F32R, at=after("x1_hi"))
        assert after("x1_lo") <= region
        scr = made["hT_hi"][0]
        lnsq = place("lnsq", [P, 2, 4, T], F32, at=scr)
        rstd = place("rstd", [P, T], F32, at=after("lnsq"))
        sgt = place("sgt", [P, 2, T], F32, at=after("rstd"))
        gact = place("gact", [P, 2, T], F32, at=after("sgt"))
        ytok = place("ytok", [P, 4, 512], F32, at=after("gact"))
        ytok8 = place("ytok8", [8, 2, 512], F32, at=after("ytok"))
        assert after("ytok8") <= made["orT_hi"][0]
        g_hi = place("g_hi", [P, HF2, T], F32R, at=after("uT"))
        g_lo = place("g_lo", [P, HF2, T], F32R, at=after("g_hi"))
        assert after("g_lo") <= made["usum"][0]

        acc = [ctx.enter_context(nc.psum_tensor(f"acc{i}", [P, 2, 512], F32)) for i in range(2)]
        X = ctx.enter_context(nc.psum_tensor("X", [P, 4, 512], F32))

        q_rows = nc.dram_tensor("q_rows", [DEC, 1024], F32, kind="Internal").ap()
        v_rows = nc.dram_tensor("v_rows", [DEC, 1024], F32, kind="Internal").ap()

        def sem(name):
            return ctx.enter_context(nc.semaphore(name))

        raw_in = [sem(f"raw_in{i}") for i in range(RING)]
        x_in = [sem(f"x_in{i}") for i in range(3)]
        y_stored = [sem(f"y_stored{i}") for i in range(4)]
        y8_stored = [sem(f"y8_stored{i}") for i in range(2)]
        page_in = [sem(f"page_in{i}") for i in range(PAGES)]
        names = """hi_made lo_made multiplied act_step dve_step ident_in cst_in parrows_in wff_in bf_in ptab_in p_in
          cst_par xn_made xn_act_made xn_scale xT_ps h_made h_hi h_lo ff_ps ln_std lsg_abs lsg_ln logf_made
          lfn_made pT_ps p_hi p_made past_in decay_ps f_evac f_ktok_ps f_ktok_sb f_score_ps f_score_sb f_exp
          f_prob f_probT_ps f_probT_sb f_vtok_ps f_vtok_sb f_o_ps f_o_hi f_o_lo f_store_k f_store_v f_decay
          snew_ps snew_made bias_made r_evac r_rope r_ps1 r_kd_sb r_st_sb r_v_ps r_v_sb r_o_ps r_o_sb r_s_ps
          r_s_sb r_mean_ps r_cen r_sq r_var_ps r_std r_y r_hi r_lo r_store_s r_store_v q_in page_used sc_made
          sc_ps s8_made e8_made p8_made p8_ps probT_made pv_ps ov_made ov_ps of_made st_in vb_in st_scaled
          st_new st_ps or_made or_ps orS_made st_stored pnew_made t_diag t_pb_ps t_of t_mean_ps t_cen t_sq
          t_var_ps t_std t_or t_hi t_lo mix_made mix_hi_made mix_lo_made u_made lnm_ps cen_made sq_made
          lnv_ps lnstd_made x1_made x1_hi_made x1_lo_made r_res g_made g_hi_made g_lo_made scaled x1_act_made
          yT_ps y_tok y8_tok acc0_free acc1_free pool_step sp_step""".split()
        S = {n: sem(n) for n in names}
        free = [S["acc0_free"], S["acc1_free"]]

        W = {k: a[k] for k in ("w_in", "w_ret_proj", "w_fox_proj", "w_out", "w1", "w3", "w2", "w_pg", "w_pe")}

        def piece(w, col, kt0, n_kt):
            def src(it):
                return w[kt0 * P:(kt0 + n_kt) * P, ds(col(it), NC)].rearrange("(t p) n -> p t n", p=P)
            return src

        def group(w, col, rhs, n_tiles, acc_i, kt_row0=0, ready=None):
            out = []
            for k in range(0, n_tiles, KT):
                n = min(KT, n_tiles - k)
                out.append(Chunk(piece(w, col, kt_row0 + k, n), rhs, k, n, acc_i, k == 0, k + n == n_tiles,
                                 ready and ready(k + n)))
            return out

        plan = {"chunks": 0, "groups": [0, 0]}
        RQ, RK, RV, RG, FQ, FK, FV, FF = (1024 * i for i in range(8))
        GR = FF + H_F
        GF = GR + D
        h = (hT_hi, hT_lo)
        w_in = W["w_in"]

        def col(start, per, off):
            return lambda it: it * per + (start + off)

        def heads(order, per, ready=None):
            out = []
            for start in order:
                for i in range(per // NC):
                    out += group(w_in, col(start, per, i * NC), h, DT, i % 2, ready=ready)
            return out
        phF = Phase(plan, 2, heads([FK, FQ, FV], 512, ready=lambda k: ("h_lo", k)))
        phR = Phase(plan, 2, heads([RK, RQ, RV, RG], 512))
        phG = Phase(plan, 4, sum((group(w_in, col(g0, 512, i * NC), h, DT, n) for i in range(2) for n, g0 in enumerate((GR, GF))), []))
        phYR = Phase(plan, 1, sum((group(W["w_ret_proj"], col(0, 0, i * NC), (orT_hi, orT_lo), 8, i % 2) for i in range(8)), []))
        phYF = Phase(plan, 4, sum((group(W["w_fox_proj"], col(0, 512, i * NC), (ofT_hi, ofT_lo), 8, i) for i in range(2)), []))
        phO = Phase(plan, 4, sum((group(W["w_out"], col(0, 512, i * NC), (mix_hi, mix_lo), DT, i,
                                        ready=lambda k: ("mix_lo_made", k // 2)) for i in range(2)), []))
        phP = Phase(plan, 2, sum((group(W["w_pg"], col(0, 1024, i * NC), (x1_hi, x1_lo), DT, 0, ready=lambda k: ("x1_lo_made", k))
                                  + group(W["w_pe"], col(0, 1024, i * NC), (pT_hi, pT_lo), 2, 1) for i in range(4)), []))

        def down_chunks(half, col0):
            return sum((group(W["w2"], col(col0, 512, i * NC), (g_hi, g_lo), HF2, i, kt_row0=half * HF2,
                              ready=lambda k: ("g_lo_made", half * HF2 // 2 + k // 2 + 1)) for i in range(2)), [])
        ffn = []
        for half in range(2):
            up = Phase(plan, HF2 // 2, sum((group(W[w], col(half * HF2 * P, NC, 0), (x1_hi, x1_lo), DT, n) for n, w in enumerate(("w1", "w3"))), []))
            down = Phase(plan, 4 - half, down_chunks(half, 0))
            ffn.append((up, down))
        phLast = Phase(plan, 1, down_chunks(1, 3 * 512))

        def r_slot(it, j):
            n = it * 2 + j // 16
            return "middle" if n else "first", (None, n)

        block = ctx.enter_context(nc.Block())

        @block.sync
        def _(sp):
            for t in range(2):
                sp.dma_start(xtok[:, t, :], a["x_prompt"][t * P:(t + 1) * P]).then_inc(x_in[t], 16)
            sp.dma_start(xtok[0:DEC, 2, :], a["x_sample"]).then_inc(x_in[2], 16)
            sp.wait_ge(x_in[1], 16)

            def load(ph, it, j):
                c, n = ph.chunks[j], ph.number(it, j)
                src = c.src(it)
                sp.wait_ge(S["lo_made"], n + 1)
                sp.sem_inc(S["sp_step"], 1)
                sp.dma_start(raw[:, j % RING, 0:c.n_kt, :], src).then_inc(raw_in[j % RING], 16)

            def stream(ph):
                with sp.Fori(0, ph.iters) as it:
                    for j in range(len(ph.chunks)):
                        load(ph, it, j)
            for ph in (phF, phR, phG):
                stream(ph)
            for j in range(len(phYR.chunks)):
                load(phYR, 0, j)
            for ph in (phYF, phO, phP):
                stream(ph)
            for up, down in ffn:
                stream(up)
                stream(down)
            for j in range(len(phLast.chunks)):
                load(phLast, 0, j)
            for q in range(4):
                cols = slice(q * 512, (q + 1) * 512)
                for t in range(2):
                    slot = (q % 2) * 2 + t
                    sp.wait_ge(S["y_tok"], q * 2 + t + 1)
                    sp.dma_start(a["y_prompt"][t * P:(t + 1) * P, cols], ytok[:, slot, :]).then_inc(y_stored[slot], 16)
                sp.wait_ge(S["y8_tok"], q + 1)
                sp.dma_start(a["y_sample"][:, cols], ytok8[:, q % 2, :]).then_inc(y8_stored[q % 2], 16)
            for i in range(4):
                sp.wait_ge(y_stored[i], 16 * 2)
            for i in range(2):
                sp.wait_ge(y8_stored[i], 16 * 2)

        def slot_uses(ph, it, j):
            n_body, c0 = len(ph.chunks) // RING, ph.chunk0 // RING
            return it * n_body + (c0 + j // RING + 1)

        def split_hi(act, ph, it, j):
            n, s, k = ph.number(it, j), j % RING, ph.n_kt(j)
            act.wait_ge(raw_in[s], slot_uses(ph, it, j) * 16)
            act.wait_ge(S["multiplied"], n + 1)
            nc.scalar.activation(whi[:, s, 0:k, :], raw[:, s, 0:k, :], ACT.Copy).then_inc(S["hi_made"], 1)

        def split_lo(dve, ph, it, j):
            n, s, k = ph.number(it, j), j % RING, ph.n_kt(j)
            dve.wait_ge(S["hi_made"], n + 1)
            nc.vector.tensor_tensor(wlo[:, s, 0:k, :], raw[:, s, 0:k, :], whi[:, s, 0:k, :].bitcast(F32),
                                    ALU.subtract).then_inc(S["lo_made"], 1)

        def group_done(eng, ph, it, j):
            eng.wait_ge(S["multiplied"], ph.number(it, j) + (RING + 1))

        def acc2(i):
            return acc[i][:, :, 0:T]

        @block.tensor
        def _(pe):
            mm, tr = nc.tensor.matmul, nc.tensor.transpose
            pe.wait_ge(S["ident_in"], 16)
            pe.wait_ge(S["parrows_in"], 16 * 7)
            tr(X[:, 0, 0:104], prow[0:104, :], ident[0:104, 0:104]).then_inc(S["cst_par"], 1)
            pe.wait_ge(S["xn_made"], 2)
            pe.wait_ge(S["xn_act_made"], 1)
            for k in range(DT):
                b = k % 4
                if k == 0:
                    pe.wait_ge(S["cst_par"], 2)
                if k >= 4:
                    pe.wait_ge(S["h_made"], k - 3)
                for t in range(2):
                    tr(X[:, b, t * P:(t + 1) * P], xtok[:, t, k * P:(k + 1) * P], ident)
                tr(X[:, b, SEQ:T], xtok[0:DEC, 2, k * P:(k + 1) * P], ident[0:DEC, 0:DEC]).then_inc(S["xT_ps"], 1)
            pe.wait_ge(S["wff_in"], 16)
            pe.wait_ge(S["h_made"], DT)
            for t, (lo, n) in enumerate(((0, P), (P, P), (SEQ, DEC))):
                for k in range(DT):
                    last = mm(X[0:n, 0, t * 8:t * 8 + 8], h32[:, k, lo:lo + n], wff[:, k, :], start=k == 0, stop=k == DT - 1)
            last.then_inc(S["ff_ps"], 1)
            pe.wait_ge(S["p_in"], 32)
            for k in range(2):
                for t in range(2):
                    tr(X[:, 1 + k, t * P:(t + 1) * P], ptok[:, t, k * P:(k + 1) * P], ident)
                last = tr(X[:, 1 + k, SEQ:T], ptok[0:DEC, 2, k * P:(k + 1) * P], ident[0:DEC, 0:DEC])
            last.then_inc(S["pT_ps"], 1)
            def multiply(ph, it, j):
                c, n, s = ph.chunks[j], ph.number(it, j), j % RING
                xh, xl = c.rhs
                if c.first:
                    pe.wait_ge(free[c.acc], ph.group(it, j) + 1)
                if c.ready:
                    pe.wait_ge(S[c.ready[0]], c.ready[1])
                pe.wait_ge(S["hi_made"], n + 1)
                for t in range(c.n_kt):
                    for m in range(2):
                        w = whi[:, s, t, m * P:(m + 1) * P]
                        mm(acc[c.acc][:, m, 0:T], w, xh[:, c.kt0 + t, :], start=c.first and t == 0, stop=False)
                        mm(acc[c.acc][:, m, 0:T], w, xl[:, c.kt0 + t, :], start=False, stop=False)
                pe.wait_ge(S["lo_made"], n + (RING + 1))
                for t in range(c.n_kt):
                    for m in range(2):
                        last = mm(acc[c.acc][:, m, 0:T], wlo[:, s, t, m * P:(m + 1) * P], xh[:, c.kt0 + t, :],
                                  start=False, stop=c.last and t == c.n_kt - 1)
                last.then_inc(S["multiplied"], 1)

            def fox_key_rows(it):
                pe.wait_ge(S["cst_in"], 16)
                pe.wait_ge(S["logf_made"], 2)
                pe.wait_ge(S["p_made"], 1)
                if it:
                    pe.wait_ge(S["lfn_made"], 2)
                pe.wait_ge(S["f_evac"], it * 6 + 4)
                for t in range(2):
                    for i in range(4):
                        tr(X[:, t, i * P:(i + 1) * P], kT4[:, i, t * P:(t + 1) * P], ident)
                for n, x in enumerate((kT4, qT4)):
                    for i in range(4):
                        last = tr(X[0:DEC, 2 + n, i * P:(i + 1) * P], x[:, i, SEQ:T], ident)
                last.then_inc(S["f_ktok_ps"], 1)

            def fox_scores(it):
                pe.wait_ge(S["f_ktok_sb"], it * 2 + 2)
                pe.wait_ge(S["f_decay"], it + 1)
                for i in range(4):
                    b = X[:, i, :]
                    mm(b[:, 0:P], qT4[:, i, 0:P], kT4[:, i, 0:P], start=True, stop=False)
                    mm(b[:, 0:P], const("le"), decay4[:, i, 0:P], start=False, stop=True)
                    mm(b[:, P:3 * P], qT4[:, i, P:SEQ], kT4[:, i, 0:SEQ], start=True, stop=False)
                    mm(b[:, P:3 * P], const("le"), decay4[:, i, P:3 * P], start=False, stop=False)
                    last = mm(b[:, P:2 * P], const("ones"), decay4[:, i, 0:P], start=False, stop=True)
                last.then_inc(S["f_score_ps"], 1)

            def fox_prob_T(it):
                pe.wait_ge(S["f_prob"], it + 1)
                for i in range(4):
                    for n in range(3):
                        last = tr(X[:, i, n * P:(n + 1) * P], prob4[:, i, n * P:(n + 1) * P], ident)
                last.then_inc(S["f_probT_ps"], 1)

            def fox_value_rows(it):
                pe.wait_ge(S["f_probT_sb"], it + 1)
                pe.wait_ge(S["f_evac"], it * 6 + 6)
                for t in range(2):
                    for i in range(4):
                        tr(X[:, t, i * P:(i + 1) * P], vT4[:, i, t * P:(t + 1) * P], ident)
                for i in range(4):
                    last = tr(X[0:DEC, 2, i * P:(i + 1) * P], vT4[:, i, SEQ:T], ident)
                last.then_inc(S["f_vtok_ps"], 1)

            def fox_out(it):
                pe.wait_ge(S["f_vtok_sb"], it * 2 + 2)
                for i in range(4):
                    o = X[:, 2 + i // 2, (i % 2) * SEQ:(i % 2 + 1) * SEQ]
                    mm(o, vtok[:, 0, i * P:(i + 1) * P], probT4[:, i, 0:SEQ], start=True, stop=False)
                    last = mm(o[:, P:SEQ], vtok[:, 1, i * P:(i + 1) * P], probT4[:, i, SEQ:3 * P], start=False, stop=True)
                last.then_inc(S["f_o_ps"], 1)

            def past_bias():
                pe.wait_ge(S["cst_in"], 16)
                pe.wait_ge(S["past_in"], 16 * DEC * NPG)
                L4 = Lc[:, :, :].rearrange("s (b p) h -> s b (p h)", b=DEC)
                D4 = X[:, 3, :].rearrange("s (b m) -> s b m", b=DEC)
                mm(D4, const("gt"), L4, start=True, stop=False)
                for s in range(1, NPG):
                    last = mm(D4[:, :, 0:(NPG - s) * H_F], const("ones"), L4[:, :, s * H_F:NPG * H_F], start=False, stop=s == NPG - 1)
                last.then_inc(S["decay_ps"], 1)
                pe.wait_ge(S["logf_made"], 2)
                tr(X[0:H_F, 0, 64:64 + DEC], logfS[:, :], ident[0:8, 0:8]).then_inc(S["lfn_made"], 1)

            for it in range(phF.iters):
                for j in range(len(phF.chunks)):
                    multiply(phF, it, j)
                    if it == 1 and j == 1:
                        fox_value_rows(0)
                    if it == 1 and j == 2:
                        fox_out(0)
                    if it == 1 and j == 6:
                        pe.wait_ge(S["f_o_lo"], 1)
                        past_bias()
                    if j == 16:
                        fox_key_rows(it)
                    if j == 17:
                        fox_scores(it)
                    if j == 21:
                        fox_prob_T(it)

            def new_scores():
                pe.wait_ge(S["f_o_lo"], 2)
                pe.wait_ge(S["snew_made"], 1)
                for b in range(DEC):
                    last = mm(X[0:H_F, 0, b:b + 1], prodS[:, b, :], const("ones")[:, 0:1], start=True, stop=True)
                last.then_inc(S["snew_ps"], 1)

            def past_scores_T(slot):
                pe.wait_ge(S["of_made"], line(slot, 1, 0))
                pe.wait_ge(S["sc_made"], line(slot, 1, 1))
                for p in range(NPG):
                    last = tr(X[0:H_F, 1 + p // 4, (p % 4) * P:(p % 4 + 1) * P], scd[:, p, :], ident)
                last.then_inc(S["sc_ps"], 1)

            def past_probs_T(slot):
                pe.wait_ge(S["of_made"], line(slot, 1, 0))
                pe.wait_ge(S["p8_made"], line(slot, 1, 0))
                for p in range(NPG):
                    last = mm(X[:, 0, p * 8:p * 8 + 8], s8[:, p * P:(p + 1) * P], ident[0:8, 0:8], start=True, stop=True)
                last.then_inc(S["p8_ps"], 1)

            def past_values(sort, slot, p):
                if p == 0:
                    pe.wait_ge(S["probT_made"], line(slot, 1, 0))
                s, fills = page_of(sort, slot, ("value", p))
                pe.wait_ge(page_in[s], fills * 16)
                for half, g in enumerate(HALVES):
                    last = mm(X[g:g + H_F, 0, :], probT[:, p, :], page[:, s, half * 512:half * 512 + 512],
                              start=p == 0, stop=p == NPG - 1)
                last.then_inc(S["pv_ps"], 1)

            def own_values(slot):
                pe.wait_ge(S["ov_made"], line(slot, 1, 0))
                for i in range(H_F):
                    g = HALVES[i // 4]
                    last = mm(X[:, i // 4 * 2, 64 + i:65 + i], ov8[g:g + H_F, i % 4 * P:(i % 4 + 1) * P], ident[g:g + H_F, g + i:g + i + 1],
                              start=True, stop=True)
                last.then_inc(S["ov_ps"], 1)

            def window(sort, slot, pos):
                if sort == "first":
                    return
                if pos == 0:
                    past_scores_T(slot)
                if pos == 4:
                    past_probs_T(slot)
                for p in range(NPG):
                    if VALUE_POS[p] == pos:
                        past_values(sort, slot, p)
                if pos == 15:
                    own_values(slot)

            def ret_scores(it):
                pe.wait_ge(S["of_made"], it * 2 + 1)
                pe.wait_ge(S["r_rope"], it * 4 + 4)
                if it == 0:
                    pe.wait_ge(S["snew_made"], 2)
                    pe.wait_ge(S["f_o_lo"], 2)
                pe.wait_ge(S["s8_made"], it * 2 + 1)
                for i in range(2):
                    for t in range(2):
                        for d in range(2):
                            tr(X[:, 3 * i, t * 256 + d * P:t * 256 + (d + 1) * P], rk2[:, i, d, t * P:(t + 1) * P], ident)
                for i in range(2):
                    for d in range(2):
                        mm(X[:, 1 + i, 0:SEQ], rk2[:, i, d, 0:P], rq2[:, i, d, 0:SEQ], start=d == 0, stop=d == 1)
                    for d in range(2):
                        last = mm(X[:, 1 + i, SEQ:3 * P], rk2[:, i, d, P:SEQ], rq2[:, i, d, P:SEQ], start=d == 0, stop=d == 1)
                last.then_inc(S["r_ps1"], 1)

            def ret_value_rows(it):
                pe.wait_ge(S["r_kd_sb"], it * 2 + 2)
                pe.wait_ge(S["r_st_sb"], it + 1)
                pe.wait_ge(free[1], phR.group(it, 23) + 2)
                for i in range(2):
                    for t in range(2):
                        for d in range(2):
                            tr(X[:, 1 + i, t * 256 + d * P:t * 256 + (d + 1) * P], rv2[:, i, d, t * P:(t + 1) * P], ident)
                for i in range(2):
                    for d in range(2):
                        last = tr(X[0:DEC, 3, i * 256 + d * P:i * 256 + (d + 1) * P], rv2[:, i, d, SEQ:T], ident)
                last.then_inc(S["r_v_ps"], 1)

            def ret_out(it):
                pe.wait_ge(S["r_v_sb"], it * 2 + 2)
                for i in range(2):
                    for e in range(2):
                        o = X[:, 1 + i, e * SEQ:(e + 1) * SEQ]
                        mm(o, vtok2[:, i, 0, e * P:(e + 1) * P], sT2[:, i, 0:SEQ], start=True, stop=False)
                        last = mm(o[:, P:SEQ], vtok2[:, i, 1, e * P:(e + 1) * P], sT2[:, i, SEQ:3 * P], start=False, stop=True)
                last.then_inc(S["r_o_ps"], 1)

            def ret_state(it, i, bank):
                for d in range(2):
                    for t in range(2):
                        last = mm(X[:, bank, d * 256:(d + 1) * 256], kdtok[:, i, t, d * P:(d + 1) * P], vtok2[:, i, t, :],
                                  start=t == 0, stop=t == 1)
                last.then_inc(S["r_s_ps"], 1)

            def ret_sum(src, bank, signal):
                for i in range(2):
                    for e in range(2):
                        last = mm(X[:, bank, i * SEQ:(i + 1) * SEQ], const("ones"), src[:, i, e, :], start=e == 0, stop=e == 1)
                last.then_inc(S[signal], 1)

            for it in range(phR.iters):
                for j in range(len(phR.chunks)):
                    multiply(phR, it, j)
                    if it == 0 and j == 1:
                        fox_value_rows(1)
                    if it == 0 and j == 2:
                        fox_out(1)
                    if it == 0 and j == 5:
                        new_scores()
                    if it and j == 0:
                        pe.wait_ge(S["r_s_sb"], it * 2)
                        pe.wait_ge(S["r_std"], it)
                    if j == 16:
                        pe.wait_ge(S["snew_made"], 2)
                        pe.wait_ge(S["f_o_lo"], 2)
                    if j == 20:
                        pe.wait_ge(S["r_kd_sb"], it * 2 + 1)
                    if j == 31:
                        pe.wait_ge(S["r_std"], it + 1)
                    window(*r_slot(it, j), j % 16)
                    if j == 18:
                        ret_scores(it)
                    if j == 24:
                        ret_value_rows(it)
                    if j == 25:
                        ret_out(it)
                    if j == 26:
                        ret_state(it, 0, 3)
                        pe.wait_ge(S["r_o_sb"], it + 1)
                        ret_state(it, 1, 1)
                        ret_sum(oR, 2, "r_mean_ps")
                    if j == 28:
                        pe.wait_ge(S["r_sq"], it + 1)
                        ret_sum(sqR, 2, "r_var_ps")

            def state_out(it, n):
                k = it * 2 + n
                pe.wait_ge(S["st_new"], k + 1)
                pe.wait_ge(S["or_made"], k + 1)
                for i in range(H_R):
                    g = HALVES[i // 2]
                    for d in range(2):
                        last = mm(X[g:g + DEC, 3, i % 2 * 256:(i % 2 + 1) * 256], rqS[:, i, d, :], stateS[:, i, d, :],
                                  start=d == 0, stop=d == 1)
                last.then_inc(S["st_ps"], 1)

            pe.wait_ge(S["r_s_sb"], 4)
            pe.wait_ge(S["r_std"], 2)
            with pe.Fori(0, phG.iters) as it:
                for j in range(len(phG.chunks)):
                    multiply(phG, it, j)
                    window("middle", (it, 4), j)
                    if j == 7:
                        state_out(it, 0)
                    if j == 14:
                        state_out(it, 1)

            pe.wait_ge(S["of_made"], DEC)
            pe.wait_ge(S["or_made"], DEC + 1)
            for i in range(H_R):
                g = HALVES[i // 2]
                for e in range(2):
                    at = i % 2 * 256 + e * P
                    last = tr(X[:, 3 - i // 2, (i * 2 + e) * DEC:(i * 2 + e + 1) * DEC], or8[g:g + DEC, at:at + P], ident[g:g + DEC, g:g + DEC])
            last.then_inc(S["or_ps"], 1)
            pe.wait_ge(S["orS_made"], 1)

            def sample_sum(src, bank, signal):
                for e in range(2):
                    last = mm(X[:, bank, 0:32], const("ones"), src[:, :, e, :], start=e == 0, stop=e == 1)
                last.then_inc(S[signal], 1)
            sample_sum(orS, 2, "t_mean_ps")
            pe.wait_ge(S["t_sq"], 1)
            sample_sum(small[:, 1, :].rearrange("p (h e b) -> p h e b", h=H_R, e=2), 3, "t_var_ps")
            pe.wait_ge(S["t_lo"], 1)
            pe.wait_ge(S["r_lo"], 4)
            for j in range(len(phYR.chunks)):
                multiply(phYR, 0, j)
                window("last", (None, DEC), j)
                if j == 5:
                    pe.wait_ge(S["t_diag"], 1)
                    mm(X[:, 3, 0:64], const("ones")[0:8, :], pdiag[:, :, :].rearrange("g h b -> g (h b)"), start=True, stop=True)\
                        .then_inc(S["t_pb_ps"], 1)
            pe.wait_ge(S["t_lo"], 2)
            pe.wait_ge(S["f_o_lo"], 2)

            def plain(ph):
                with pe.Fori(0, ph.iters) as it:
                    for j in range(len(ph.chunks)):
                        multiply(ph, it, j)
            plain(phYF)
            plain(phO)

            def norm_sums(n):
                pe.wait_ge(S["u_made"], 4 * (n + 1))
                for m in range(2):
                    last = mm(X[:, 0, 0:T], const("ones"), usum[:, m, :], start=m == 0, stop=m == 1)
                last.then_inc(S["lnm_ps"], 1)
                for q in range(4):
                    pe.wait_ge(S["sq_made"], 4 * n + q + 1)
                    for k in range(4):
                        last = mm(X[:, 1, 0:T], const("ones"), lnsq[:, q % 2, k, :], start=q == 0 and k == 0, stop=q == 3 and k == 3)
                    last.then_inc(S["lnv_ps"], 1)
            norm_sums(0)
            plain(phP)
            for up, down in ffn:
                plain(up)
                plain(down)
            for j in range(len(phLast.chunks)):
                multiply(phLast, 0, j)
            norm_sums(1)
            for q in range(4):
                pe.wait_ge(S["x1_made"], 8 + q * 2 + 2)
                pe.wait_ge(S["x1_act_made"], 8 + q * 2 + 2)
                for t, n in enumerate((P, P, DEC)):
                    k3 = q * 3 + t
                    if k3 >= 4:
                        b, u = divmod(k3 - 4, 3)
                        if u == 2:
                            pe.wait_ge(S["y8_tok"], b + 1)
                        else:
                            pe.wait_ge(S["y_tok"], b * 2 + u + 1)
                    for k in range(4):
                        last = tr(X[0:n, k3 % 4, k * P:(k + 1) * P], uT[:, q * 4 + k, t * P:t * P + n], ident)
                    last.then_inc(S["yT_ps"], 1)

        @block.scalar
        def _(act):
            A = nc.scalar.activation
            link = Chain(act, S["act_step"])
            n_first = where["eps"][0] + 2
            act.dma_start(cst[:, 0:n_first], a["shape_constants"][:, 0:n_first]).then_inc(S["ident_in"], 16)
            for n, name in enumerate(("ln_emb_g", "ln_emb_b", "ln1_g", "ln1_b", "ln2_g", "ln2_b")):
                act.dma_start(prow[n * 16:(n + 1) * 16, :], a[name].rearrange("(r c) -> r c", c=P)).then_inc(S["parrows_in"], 16)
            act.dma_start(prow[96:104, :], a["gn_g"].rearrange("(r c) -> r c", c=P)).then_inc(S["parrows_in"], 16)
            act.wait_ge(x_in[1], 16)
            act.dma_start(cst[:, n_first:n_const], a["shape_constants"][:, n_first:n_const]).then_inc(S["cst_in"], 16)
            act.dma_start(wff[:, :, :], a["w_in"][:, FF:FF + H_F].rearrange("(t p) n -> p t n", p=P)).then_inc(S["wff_in"], 16)
            act.dma_start(bf[:, :], a["b_f"].rearrange("(o n) -> o n", o=1).partition_broadcast(P)).then_inc(S["bf_in"], 16)
            act.dma_start(ptok[:, 0:2, :], a["p_prompt"].rearrange("(t p) d -> p t d", p=P)).then_inc(S["p_in"], 16)
            act.dma_start(ptok[0:DEC, 2, :], a["p_sample"]).then_inc(S["p_in"], 16)
            act.wait_ge(S["ident_in"], 16)
            act.wait_ge(S["ln_std"], 3)
            eps_ln, eps_gn = const("eps")[:, 0:1], const("eps")[:, 1:2]
            for t, n in enumerate((P, P, DEC)):
                last = A(stat[0:n, 40 + t:41 + t], stat[0:n, 32 + 2 * t + 1:32 + 2 * t + 2], ACT.Sqrt, bias=eps_ln[0:n, :])
            last.then_inc(S["ln_std"], 1)
            act.wait_ge(S["xn_scale"], 1)
            A(xtok[:, 1, :], xtok[:, 1, :], ACT.Identity, bias=stat[:, 48:49], scale=stat[:, 45:46]).then_inc(S["xn_act_made"], 1)
            for k in range(DT):
                act.wait_ge(S["h_made"], k + 1)
                A(hT_hi[:, k, :], h32[:, k, :], ACT.Copy).then_inc(S["h_hi"], 1)
                if k % 6 == 5 and k // 6 < 1:
                    split_hi(act, phF, 0, 0)
            for j in range(1, AHEAD):
                split_hi(act, phF, 0, j)
            act.wait_ge(S["cst_in"], 16)
            act.wait_ge(S["lsg_abs"], 1)
            link.step(A(stat[:, 0:16], stat[:, 0:16], ACT.Exp, scale=-1.0))
            link.step(A(small[0:8, 3, 0:8], small[0:8, 3, 0:8], ACT.Exp, scale=-1.0))
            A(stat[:, 0:16], stat[:, 0:16], ACT.Ln, bias=1.0)
            A(small[0:8, 3, 0:8], small[0:8, 3, 0:8], ACT.Ln, bias=1.0).then_inc(S["lsg_ln"], 1)
            act.wait_ge(S["pT_ps"], 1)
            A(pT_hi[:, :, :], X[:, 1:3, 0:T], ACT.Copy).then_inc(S["p_hi"], 1)

            def fox_values(it):
                act.wait_ge(S["f_vtok_ps"], it + 1)
                if it:
                    act.wait_ge(S["f_store_v"], it * 32)
                A(vtok[:, :, :], X[:, 0:2, :], ACT.Copy).then_inc(S["f_vtok_sb"], 1)
                A(vs8[:, :], X[0:DEC, 2, :], ACT.Copy).then_inc(S["f_vtok_sb"], 1)

            def fox_result(it):
                act.wait_ge(S["f_o_ps"], it + 1)
                A(ofT_hi[:, it * 4:it * 4 + 4, 0:SEQ], X[:, 2:4, :].rearrange("p b (i t) -> p (b i) t", i=2), ACT.Copy)\
                    .then_inc(S["f_o_hi"], 1)

            for it in range(phF.iters):
                for j in range(len(phF.chunks)):
                    split_hi(act, phF, it, j + AHEAD)
                    if phF.chunks[j].last:
                        g = j // 4
                        dst, src_s, i0 = ((kT4, kS, 0), (kT4, kS, 2), (qT4, qS, 0), (qT4, qS, 2), (vT4, vS, 0), (vT4, vS, 2))[g]
                        group_done(act, phF, it, j)
                        ac = phF.chunks[j].acc
                        A(dst[:, i0:i0 + 2, :], acc2(ac), ACT.Copy, scale=QS if dst is qT4 else 1.0).then_inc(free[ac], 1)
                        act.wait_ge(free[ac], phF.group(it, j) + 2)
                        A(src_s[:, it * 4 + i0:it * 4 + i0 + 2, :], dst[:, i0:i0 + 2, SEQ:T], ACT.Copy).then_inc(S["f_evac"], 1)
                    if it == 1 and j == 1:
                        fox_values(0)
                    if it == 1 and j == 2:
                        fox_result(0)
                    if j == 16:
                        act.wait_ge(S["f_ktok_ps"], it + 1)
                        if it:
                            act.wait_ge(S["f_store_k"], it * 48)
                        A(ktok[:, :, :], X[:, 0:2, :], ACT.Copy).then_inc(S["f_ktok_sb"], 1)
                        A(kqs[:, :, :], X[0:DEC, 2:4, :], ACT.Copy).then_inc(S["f_ktok_sb"], 1)
                    if j == 17:
                        act.wait_ge(S["f_score_sb"], it + 1)
                        for i in range(4):
                            A(prob4[:, i, 0:P], prob4[:, i, 0:P], ACT.Exp, bias=softs[:, i:i + 1], accum_out=softs[:, 8 + i:9 + i])
                            last = A(prob4[:, i, P:3 * P], prob4[:, i, P:3 * P], ACT.Exp, bias=softs[:, 4 + i:5 + i],
                                     accum_out=softs[:, 12 + i:13 + i])
                        last.then_inc(S["f_exp"], 1)
                    if j == 21:
                        act.wait_ge(S["f_probT_ps"], it + 1)
                        A(probT4[:, :, :], X[:, :, 0:3 * P], ACT.Copy).then_inc(S["f_probT_sb"], 1)

            def window(sort, slot, pos):
                if sort != "first" and pos == 1:
                    act.wait_ge(S["s8_made"], line(slot, 1, 0))
                    A(s8[:, 0:1025], s8[:, 0:1025], ACT.Exp, bias=softs[0:8, 20:21], accum_out=softs[0:8, 21:22])\
                        .then_inc(S["e8_made"], 1)
                if sort != "first" and pos == 14:
                    act.wait_ge(S["of_made"], line(slot, 1, 0))
                    act.wait_ge(S["pv_ps"], line(slot, NPG, 1))
                    for g in HALVES:
                        last = A(ov8[g:g + H_F, :], X[g:g + H_F, 0, :], ACT.Copy)
                    last.then_inc(S["ov_made"], 1)

            def ret_result(it, i):
                act.wait_ge(S["r_y"], it * 2 + i + 1)
                k = (it * 2 + i) * 2
                A(orT_hi[:, k:k + 2, 0:SEQ], oR[:, i, :, :], ACT.Copy).then_inc(S["r_hi"], 1)

            for it in range(phR.iters):
                for j in range(len(phR.chunks)):
                    split_hi(act, phR, it, j + AHEAD)
                    if it == 0 and j == 1:
                        fox_values(1)
                    if it == 0 and j == 2:
                        fox_result(1)
                    window(*r_slot(it, j), j % 16)
                    if it and j == 1:
                        ret_result(it - 1, 1)
                    if j == 30:
                        ret_result(it, 0)
                    if phR.chunks[j].last and j >= 16:
                        g = j // 4 - 4
                        ac = phR.chunks[j].acc
                        group_done(act, phR, it, j)
                        if g < 2:
                            A(rv2[:, g, :, :], acc2(ac), ACT.Copy).then_inc(free[ac], 1)
                        else:
                            if it:
                                act.wait_ge(S["r_y"], it * 2)
                            A(sg2[:, g - 2, :, :], acc2(ac), ACT.Silu).then_inc(free[ac], 1)
                            act.wait_ge(free[ac], phR.group(it, j) + 2)
                            A(sgS[:, it * 2 + g - 2, :, :], sg2[:, g - 2, :, SEQ:T], ACT.Copy).then_inc(S["r_evac"], 1)
                    if j == 18:
                        act.wait_ge(S["r_ps1"], it + 1)
                        kd0 = where["kdec"][0] + it * 4
                        for i in range(2):
                            for t in range(2):
                                last = A(kdtok[:, i, t, :], X[:, 3 * i, t * 256:(t + 1) * 256], ACT.Copy,
                                         scale=cst[:, kd0 + i * 2 + t:kd0 + i * 2 + t + 1])
                            last.then_inc(S["r_kd_sb"], 1)
                        A(rkS[:, it * 2:it * 2 + 2, :, :].rearrange("p h d b -> p (h d) b"),
                          rk2[:, :, :, SEQ:T].rearrange("p h d b -> p (h d) b"), ACT.Copy, scale=1.0 / 16.0)
                        A(rqS[:, it * 2:it * 2 + 2, :, :].rearrange("p h d b -> p (h d) b"),
                          rq2[:, :, :, SEQ:T].rearrange("p h d b -> p (h d) b"), ACT.Copy)
                    if j == 24:
                        act.wait_ge(S["r_v_ps"], it + 1)
                        if it:
                            act.wait_ge(S["r_store_v"], it * 16)
                        else:
                            act.wait_ge(S["f_store_v"], 64)
                        A(vtok2[:, :, :, :].rearrange("p h t c -> p h (t c)"), X[:, 1:3, :], ACT.Copy).then_inc(S["r_v_sb"], 1)
                        A(vr8[:, :], X[0:DEC, 3, :], ACT.Copy).then_inc(S["r_v_sb"], 1)
                    if j == 25:
                        act.wait_ge(S["r_o_ps"], it + 1)
                        if it:
                            act.wait_ge(S["r_lo"], it * 2)
                        A(oR[:, :, :, :].rearrange("p h e t -> p h (e t)"), X[:, 1:3, :], ACT.Copy).then_inc(S["r_o_sb"], 1)
                    if j == 26:
                        for i, bank in ((0, 3), (1, 1)):
                            act.wait_ge(S["r_s_ps"], it * 2 + i + 1)
                            A(stR[:, i, :], X[:, bank, :], ACT.Copy).then_inc(S["r_s_sb"], 1)
                    if j == 27:
                        act.wait_ge(S["r_cen"], it + 1)
                        A(sqR[:, :, :, :].rearrange("p h e t -> p (h e t)"), oR[:, :, :, :].rearrange("p h e t -> p (h e t)"), ACT.Square)\
                            .then_inc(S["r_sq"], 1)
                    if j == 28:
                        act.wait_ge(S["r_var_ps"], it + 1)
                        A(sqR[:, :, 0, :], X[:, 2, :].rearrange("p (h t) -> p h t", h=2), ACT.Sqrt, bias=eps_gn, scale=1.0 / 256.0)\
                            .then_inc(S["r_std"], 1)
            ret_result(1, 1)

            def state_scale(it, n):
                k = it * 2 + n
                act.wait_ge(S["st_in"], k * 16 + 16)
                for i in range(H_R):
                    last = A(stateS[:, i, :, :].rearrange("p d e -> p (d e)"), stateS[:, i, :, :].rearrange("p d e -> p (d e)"),
                             ACT.Copy, scale=gammas[i])
                last.then_inc(S["st_scaled"], 1)

            act.wait_ge(S["r_lo"], 4)
            act.wait_ge(S["r_store_s"], 32)
            act.wait_ge(S["r_store_v"], 32)
            with act.Fori(0, phG.iters) as it:
                for j in range(len(phG.chunks)):
                    split_hi(act, phG, it, j + AHEAD)
                    window("middle", (it, 4), j)
                    if phG.chunks[j].last:
                        g, ac = j // 4, phG.chunks[j].acc
                        group_done(act, phG, it, j)
                        A(gate[:, ds(it * 4 + g // 2 * 2, 2), ac, :], acc2(ac), ACT.Sigmoid).then_inc(free[ac], 1)
                    if j == 2:
                        state_scale(it, 0)
                    if j == 10:
                        state_scale(it, 1)

            act.wait_ge(S["t_cen"], 1)
            A(small[:, 1, :], orS[:, :, :, :].rearrange("p h e b -> p (h e b)"), ACT.Square).then_inc(S["t_sq"], 1)
            act.wait_ge(S["t_var_ps"], 1)
            A(small[:, 2, 0:32], X[:, 3, 0:32], ACT.Sqrt, bias=eps_gn, scale=1.0 / 256.0).then_inc(S["t_std"], 1)
            act.wait_ge(S["t_or"], 1)
            A(orT_hi[:, :, SEQ:T], orS[:, :, :, :].rearrange("p h e b -> p (h e) b"), ACT.Copy).then_inc(S["t_hi"], 1)

            for j in range(len(phYR.chunks)):
                split_hi(act, phYR, 0, j + AHEAD)
                window("last", (None, DEC), j)
            act.wait_ge(S["t_of"], 1)
            A(ofT_hi[:, :, SEQ:T], small[:, 0, :].rearrange("p (h b) -> p h b", h=H_F), ACT.Copy).then_inc(S["t_hi"], 1)
            act.wait_ge(S["st_stored"], 32 + 16 * DEC)
            with act.Fori(0, phYF.iters) as it:
                for j in range(len(phYF.chunks)):
                    split_hi(act, phYF, it, j + AHEAD)
                    if phYF.chunks[j].last:
                        act.wait_ge(S["mix_made"], it * 2 + (j // 2 + 1))
                        k = it * 4 + j // 2 * 2
                        A(mix_hi[:, ds(k, 2), :], gate[:, ds(k, 2), 0, :], ACT.Copy).then_inc(S["mix_hi_made"], 1)
            with act.Fori(0, phO.iters) as it:
                for j in range(len(phO.chunks)):
                    split_hi(act, phO, it, j + AHEAD)

            def norm(n):
                for q in range(4):
                    act.wait_ge(S["cen_made"], 4 * n + q + 1)
                    if q >= 2:
                        act.wait_ge(S["lnv_ps"], 4 * n + q - 1)
                    A(lnsq[:, q % 2, :, :], uT[:, q * 4:q * 4 + 4, :], ACT.Square).then_inc(S["sq_made"], 1)
                act.wait_ge(S["lnv_ps"], 4 * n + 4)
                A(rstd[:, :], X[:, 1, 0:T], ACT.Sqrt, bias=eps_ln, scale=1.0 / D).then_inc(S["lnstd_made"], 1)

            def gain(n, q, g0):
                act.wait_ge(S["scaled"], 4 * n + q + 1)
                for k in (q * 4 + 2, q * 4 + 3):
                    A(uT[:, k, :], uT[:, k, :], ACT.Identity, bias=par[:, g0 + 16 + k:g0 + 17 + k], scale=par[:, g0 + k:g0 + k + 1])\
                        .then_inc(S["x1_act_made"], 1)

            norm(0)
            for q in range(4):
                gain(0, q, 32)
                for k in range(q * 4, q * 4 + 4):
                    if k % 4 < 2:
                        act.wait_ge(S["x1_made"], q * 2 + k % 4 + 1)
                    else:
                        act.wait_ge(S["x1_act_made"], q * 2 + k % 4 - 1)
                    A(x1_hi[:, k, :], uT[:, k, :], ACT.Copy).then_inc(S["x1_hi_made"], 1)

            with act.Fori(0, phP.iters) as it:
                for j in range(len(phP.chunks)):
                    split_hi(act, phP, it, j + AHEAD)
                    if j % 5 == 3:
                        group_done(act, phP, it, j)
                        act.wait_ge(S["r_res"], it * 4 + j // 5 + 1)
                        A(sgt[:, :, :], acc2(0), ACT.Sigmoid).then_inc(free[0], 1)
            for half, (up, down) in enumerate(ffn):
                with act.Fori(0, up.iters) as it:
                    for j in range(len(up.chunks)):
                        split_hi(act, up, it, j + AHEAD)
                        if j == 3:
                            group_done(act, up, it, j)
                            act.wait_ge(S["g_lo_made"], it + half * HF2 // 2 + 1)
                            A(gact[:, :, :], acc2(0), ACT.Silu).then_inc(free[0], 1)
                        if j == 7:
                            act.wait_ge(S["g_made"], it + (half * HF2 // 2 + 1))
                            A(g_hi[:, ds(it * 2, 2), :], gact[:, :, :], ACT.Copy).then_inc(S["g_hi_made"], 1)
                with act.Fori(0, down.iters) as it:
                    for j in range(len(down.chunks)):
                        split_hi(act, down, it, j + AHEAD)
            for j in range(AHEAD, len(phLast.chunks)):
                split_hi(act, phLast, 0, j)
            norm(1)

            def y_rows(q):
                for t in range(2):
                    act.wait_ge(S["yT_ps"], q * 3 + t + 1)
                    if q >= 2:
                        act.wait_ge(y_stored[(q % 2) * 2 + t], 16 * (q // 2))
                    A(ytok[:, (q % 2) * 2 + t, :], X[:, (q * 3 + t) % 4, :], ACT.Copy).then_inc(S["y_tok"], 1)
            for q in range(4):
                gain(1, q, 64)
                if q >= 1:
                    y_rows(q - 1)
            y_rows(3)

        @block.vector
        def _(dve):
            V = nc.vector
            link = Chain(dve, S["dve_step"])
            for name, n in CREDIT.items():
                dve.sem_inc(S[name], n)
            for t, n in enumerate((P, P, DEC)):
                dve.wait_ge(x_in[t], 16)
                for q in range(4):
                    ins = V.bn_stats(small[0:n, t, q * 6:q * 6 + 6], xtok[0:n, t, q * 512:(q + 1) * 512])
                link.step(ins)
                V.bn_aggr(stat[0:n, 32 + 2 * t:34 + 2 * t], small[0:n, t, 0:24]).then_inc(S["ln_std"], 1)
            dve.wait_ge(S["ln_std"], 4)
            for t, n in enumerate((P, P, DEC)):
                ins = V.reciprocal(stat[0:n, 44 + t:45 + t], stat[0:n, 40 + t:41 + t])
            link.step(ins)
            V.scalar_tensor_tensor(out=stat[:, 48:49], in0=stat[:, 34:35], scalar=-1.0, in1=stat[:, 45:46], op0=ALU.mult, op1=ALU.mult)\
                .then_inc(S["xn_scale"], 1)
            for t, n in ((0, P), (2, DEC)):
                V.tensor_scalar(xtok[0:n, t, :], xtok[0:n, t, :], stat[0:n, 32 + 2 * t:33 + 2 * t], stat[0:n, 44 + t:45 + t],
                                ALU.subtract, ALU.mult).then_inc(S["xn_made"], 1)
            dve.wait_ge(S["cst_par"], 1)
            V.tensor_copy(par[:, :], X[:, 0, 0:104]).then_inc(S["cst_par"], 1)
            dve.wait_ge(S["cst_par"], 2)
            for k in range(DT):
                dve.wait_ge(S["xT_ps"], k + 1)
                V.tensor_scalar(h32[:, k, :], X[:, k % 4, 0:T], par[:, k:k + 1], par[:, 16 + k:17 + k], ALU.mult, ALU.add)\
                    .then_inc(S["h_made"], 1)
            for j in range(AHEAD):
                split_lo(dve, phF, 0, j)
            dve.wait_ge(S["h_lo"], DT)
            dve.wait_ge(S["ff_ps"], 1)
            dve.wait_ge(S["bf_in"], 16)
            zt, zs = stat[:, 16:32], small[0:8, 3, 8:16]
            V.tensor_tensor(zt.rearrange("p (t h) -> p t h", t=2), X[:, 0, 0:16].rearrange("p (t h) -> p t h", t=2),
                            bf[:, :].unsqueeze(1).broadcast_to([P, 2, H_F]), ALU.add)
            link.step(V.tensor_tensor(zs, X[0:8, 0, 16:24], bf[0:8, :], ALU.add))
            V.tensor_scalar(stat[:, 0:16], zt, -1.0, None, ALU.mult)
            link.step(V.tensor_scalar(small[0:8, 3, 0:8], zs, -1.0, None, ALU.mult))
            V.tensor_tensor(stat[:, 0:16], stat[:, 0:16], zt, ALU.max)
            link.step(V.tensor_tensor(small[0:8, 3, 0:8], small[0:8, 3, 0:8], zs, ALU.max))
            V.tensor_scalar(zt, zt, 0.0, None, ALU.min)
            V.tensor_scalar(zs, zs, 0.0, None, ALU.min).then_inc(S["lsg_abs"], 1)
            dve.wait_ge(S["lsg_ln"], 1)
            dve.wait_ge(S["lsg_abs"], 1)
            V.tensor_tensor(logf_tok[:, :, :].rearrange("p t h -> p (t h)"), zt, stat[:, 0:16], ALU.subtract).then_inc(S["logf_made"], 1)
            V.tensor_tensor(logfS[:, :], zs, small[0:8, 3, 0:8], ALU.subtract).then_inc(S["logf_made"], 1)
            dve.wait_ge(S["p_hi"], 1)
            V.tensor_tensor(pT_lo[:, :, :], X[:, 1:3, 0:T], pT_hi[:, :, :].bitcast(F32), ALU.subtract).then_inc(S["p_made"], 1)
            dve.wait_ge(S["logf_made"], 2)
            def fox_result(it):
                dve.wait_ge(S["f_o_hi"], it + 1)
                V.tensor_tensor(ofT_lo[:, it * 4:it * 4 + 4, 0:SEQ], X[:, 2:4, :].rearrange("p b (i t) -> p (b i) t", i=2),
                                ofT_hi[:, it * 4:it * 4 + 4, 0:SEQ].bitcast(F32), ALU.subtract).then_inc(S["f_o_lo"], 1)

            for it in range(phF.iters):
                for j in range(len(phF.chunks)):
                    split_lo(dve, phF, it, j + AHEAD)
                    if it == 1 and j == 2:
                        fox_result(0)
                    if it == 1 and j == 6:
                        dve.wait_ge(S["decay_ps"], 1)
                        V.tensor_copy(bias_past[:, :, :, :].rearrange("s b p h -> s (b p h)"), X[:, 3, :]).then_inc(S["bias_made"], 1)
                        dve.wait_ge(S["lfn_made"], 1)
                        V.tensor_copy(lfn8[:, :], X[0:8, 0, 64:72]).then_inc(S["lfn_made"], 1)
                    if j == 8:
                        dve.wait_ge(S["cst_in"], 16)
                        link.step(V.tensor_copy(lf4[:, :, :], logf_tok[:, :, it * 4:it * 4 + 4]))
                        V.tensor_tensor(decay4[:, :, 0:P], const("gt").unsqueeze(1).broadcast_to([P, 4, P]),
                                        lf4[:, 0, :].unsqueeze(2).broadcast_to([P, 4, P]), ALU.mult)
                        at = where["ones"][0]
                        V.tensor_tensor(decay4[:, :, P:3 * P], cst[:, at:at + 256].unsqueeze(1).broadcast_to([P, 4, 256]),
                                        lf4[:, 1, :].unsqueeze(2).broadcast_to([P, 4, 256]), ALU.mult).then_inc(S["f_decay"], 1)
                    if j == 17:
                        dve.wait_ge(S["f_score_ps"], it + 1)
                        link.step(V.tensor_tensor(prob4[:, :, :], X[:, :, 0:3 * P], const("mask").unsqueeze(1).broadcast_to([P, 4, 3 * P]), ALU.add))
                        V.tensor_reduce(softs[:, 0:4], prob4[:, :, 0:P], axis=AX.X, op=ALU.max)
                        link.step(V.tensor_reduce(softs[:, 4:8], prob4[:, :, P:3 * P], axis=AX.X, op=ALU.max))
                        V.tensor_scalar(softs[:, 0:8], softs[:, 0:8], -1.0, None, ALU.mult).then_inc(S["f_score_sb"], 1)
                    if j == 18:
                        dve.wait_ge(S["f_exp"], it + 1)
                        link.step(V.reciprocal(softs[:, 8:16], softs[:, 8:16]))
                        V.tensor_tensor(prob4[:, :, 0:P], prob4[:, :, 0:P], softs[:, 8:12].unsqueeze(2).broadcast_to([P, 4, P]), ALU.mult)
                        V.tensor_tensor(prob4[:, :, P:3 * P], prob4[:, :, P:3 * P], softs[:, 12:16].unsqueeze(2).broadcast_to([P, 4, 2 * P]), ALU.mult)\
                            .then_inc(S["f_prob"], 1)

            def new_scores():
                dve.wait_ge(S["f_evac"], 12)
                V.tensor_tensor(prodS[:, :, :].rearrange("p b h -> p h b"), qS[:, :, :], kS[:, :, :], ALU.mult).then_inc(S["snew_made"], 1)
                dve.wait_ge(S["snew_ps"], 1)
                V.tensor_copy(snew8[:, :], X[0:8, 0, 0:DEC]).then_inc(S["snew_made"], 1)

            def window(sort, slot, pos):
                if pos == 0 and sort != "first":
                    if slot[0] is None and slot[1] == 1:
                        dve.wait_ge(S["bias_made"], 1)
                        dve.wait_ge(S["lfn_made"], 2)
                        dve.wait_ge(S["snew_made"], 2)
                    dve.wait_ge(S["page_used"], line(slot, NPG * H_F, HEADS))
                    dve.wait_ge(S["sc_ps"], line(slot, 1, 0))
                    V.tensor_tensor(scd[:, :, :].rearrange("s p h -> s (p h)"), sc8[:, :, :].rearrange("s p h -> s (p h)"),
                                    bias_past[:, ds(line(slot, 1, -1), 1), :, :].rearrange("s o p h -> s (o p h)"), ALU.add)\
                        .then_inc(S["sc_made"], 1)
                if pos in KEY_POS and sort != "last":
                    p = KEY_POS.index(pos)
                    s, fills = page_of(sort, slot, ("key", p))
                    if p == 0:
                        dve.wait_ge(S["q_in"], line(slot, 16, 16))
                        dve.wait_ge(S["sc_made"], line(slot, 1, 1))
                    dve.wait_ge(page_in[s], fills * 16)
                    for i in range(H_F):
                        dve.wait_ge(S["page_used"], line(slot, NPG * H_F, p * H_F + i + 1))
                        V.tensor_tensor_reduce(out=pagesum[:, i % HEADS, :], in0=page[:, s, i * P:(i + 1) * P],
                                               in1=qbc[:, i * P:(i + 1) * P], scale=1.0, scalar=0.0, op0=ALU.mult, op1=ALU.add,
                                               accum_out=sc8[:, p, i:i + 1]).then_inc(S["page_used"], 1)
                if sort == "first":
                    return
                if pos == 1:
                    w = ds(line(slot, 1, -1), 1)
                    dve.wait_ge(S["sc_ps"], line(slot, 1, 1))
                    V.tensor_scalar(s8[:, 0:1024], X[0:8, 1:3, :].rearrange("h b c -> h (b c)"), lfn8[:, w], None, ALU.add)
                    link.step(V.tensor_copy(s8[:, 1024:1025], snew8[:, w]))
                    link.step(V.tensor_reduce(softs[0:8, 20:21], s8[:, 0:1025], axis=AX.X, op=ALU.max))
                    V.tensor_scalar(softs[0:8, 20:21], softs[0:8, 20:21], -1.0, None, ALU.mult).then_inc(S["s8_made"], 1)
                if pos == 2:
                    w = ds(line(slot, 1, -1), 1)
                    dve.wait_ge(S["e8_made"], line(slot, 1, 0))
                    link.step(V.reciprocal(softs[0:8, 21:22], softs[0:8, 21:22]))
                    V.tensor_scalar(s8[:, 0:1025], s8[:, 0:1025], softs[0:8, 21:22], None, ALU.mult).then_inc(S["p8_made"], 1)
                    dve.wait_ge(S["p8_made"], line(slot, 1, 0))
                    V.tensor_copy(pnew8[:, w], s8[:, 1024:1025]).then_inc(S["pnew_made"], 1)
                if pos == 4:
                    dve.wait_ge(S["p8_ps"], line(slot, 1, 0))
                    V.tensor_copy(probT[:, :, :].rearrange("s p h -> s (p h)"), X[:, 0, 0:64]).then_inc(S["probT_made"], 1)
                if pos == 15:
                    dve.wait_ge(S["ov_ps"], line(slot, 1, 0))
                    for half in range(2):
                        last = V.tensor_copy(ofS[:, half * 4:half * 4 + 4, ds(line(slot, 1, -1), 1)].rearrange("p h o -> p (h o)"),
                                             X[:, half * 2, 64 + half * 4:68 + half * 4])
                    last.then_inc(S["of_made"], 1)

            def rope(ph, it, j, dst):
                ac = ph.chunks[j].acc
                group_done(dve, ph, it, j)
                z = acc2(ac)
                V.tensor_tensor(dst, z, const("cos").unsqueeze(1).broadcast_to([P, 2, T]), ALU.mult)
                V.tensor_tensor(sqR2[:, 0, :], z[:, 1, :], const("nsin"), ALU.mult)
                V.tensor_tensor(sqR2[:, 1, :], z[:, 0, :], const("psin"), ALU.mult).then_inc(free[ac], 1)
                dve.wait_ge(free[ac], ph.group(it, j) + 2)
                V.tensor_tensor(dst, dst, sqR2[:, :, :], ALU.add).then_inc(S["r_rope"], 1)
                dve.wait_ge(S["r_rope"], it * 4 + (j // 4 + 1))

            sqR2 = stR[:, :, :].rearrange("p a b -> p (a b)")[:, 0:2 * T].rearrange("p (a b) -> p a b", a=2)
            dm0 = where["dmask"][0]
            def ret_result(it, i):
                dve.wait_ge(S["r_evac"], it * 2 + i + 1)
                for e in range(2):
                    k = 96 + it * 4 + i * 2 + e
                    last = V.scalar_tensor_tensor(out=oR[:, i, e, :], in0=oR[:, i, e, :], scalar=par[:, k:k + 1],
                                                  in1=sg2[:, i, e, 0:SEQ], op0=ALU.mult, op1=ALU.mult)
                last.then_inc(S["r_y"], 1)

            def ret_result_lo(it, i):
                dve.wait_ge(S["r_hi"], it * 2 + i + 1)
                k = (it * 2 + i) * 2
                V.tensor_tensor(orT_lo[:, k:k + 2, 0:SEQ], oR[:, i, :, :], orT_hi[:, k:k + 2, 0:SEQ].bitcast(F32), ALU.subtract)\
                    .then_inc(S["r_lo"], 1)

            for it in range(phR.iters):
                for j in range(len(phR.chunks)):
                    split_lo(dve, phR, it, j + AHEAD)
                    if it == 0 and j == 2:
                        fox_result(1)
                    if it == 0 and j == 3:
                        dve.wait_ge(S["f_store_k"], 96)
                    if it == 0 and j == 5:
                        new_scores()
                    if phR.chunks[j].last and j < 16:
                        g = j // 4
                        if g == 0 and it:
                            dve.wait_ge(S["r_store_s"], it * 16)
                        rope(phR, it, j, (rk2, rk2, rq2, rq2)[g][:, g % 2, :, :])
                    window(*r_slot(it, j), j % 16)
                    if it and j == 1:
                        ret_result(it - 1, 1)
                    if it and j == 2:
                        ret_result_lo(it - 1, 1)
                    if j == 18:
                        dve.wait_ge(S["r_ps1"], it + 1)
                        dm = cst[:, dm0 + it * 512:dm0 + it * 512 + 512].rearrange("p (h t) -> p h t", h=2)
                        V.tensor_tensor(sT2[:, :, 0:SEQ], X[:, 1:3, 0:SEQ], dm, ALU.mult)
                        V.tensor_tensor(sT2[:, :, SEQ:3 * P], X[:, 1:3, SEQ:3 * P], dm[:, :, 0:P], ALU.mult).then_inc(S["r_st_sb"], 1)
                    if j == 26:
                        dve.wait_ge(S["r_mean_ps"], it + 1)
                        dve.wait_ge(S["r_o_sb"], it + 1)
                        for e in range(2):
                            last = V.scalar_tensor_tensor(out=oR[:, :, e, :], in0=X[:, 2, :].rearrange("p (h t) -> p h t", h=2),
                                                          scalar=-1.0 / 256.0, in1=oR[:, :, e, :], op0=ALU.mult, op1=ALU.add)
                        last.then_inc(S["r_cen"], 1)
                    if j == 29:
                        dve.wait_ge(S["r_std"], it + 1)
                        link.step(V.reciprocal(sqR[:, :, 1, :], sqR[:, :, 0, :]))
                    if j == 30:
                        link.step(V.tensor_tensor(oR[:, :, :, :], oR[:, :, :, :], sqR[:, :, 1:2, :].broadcast_to([P, 2, 2, SEQ]), ALU.mult))
                        ret_result(it, 0)
                    if j == 31:
                        ret_result_lo(it, 0)
            ret_result(1, 1)
            ret_result_lo(1, 1)

            def state_new(it, n):
                k = it * 2 + n
                dve.wait_ge(S["st_scaled"], k + 1)
                dve.wait_ge(S["vb_in"], k * 16 + 16)
                link.step(V.tensor_copy(rk1[:, :, :, :], rkS[:, :, :, ds(k, 1)]))
                for i in range(H_R):
                    for d in range(2):
                        last = V.scalar_tensor_tensor(out=stateS[:, i, d, :], in0=vbc[:, i, :], scalar=rk1[:, i, d, :],
                                                      in1=stateS[:, i, d, :], op0=ALU.mult, op1=ALU.add)
                last.then_inc(S["st_new"], 1)

            def state_read(it, n):
                k = it * 2 + n
                dve.wait_ge(S["st_ps"], k + 2)
                dve.wait_ge(S["or_made"], k + 1)
                for g in HALVES:
                    last = V.scalar_tensor_tensor(out=or8[g:g + DEC, :], in0=X[g:g + DEC, 3, :], scalar=ident[g:g + DEC, ds(k + g, 1)],
                                                  in1=or8[g:g + DEC, :], op0=ALU.mult, op1=ALU.add)
                last.then_inc(S["or_made"], 1)

            for g in HALVES:
                ins = V.memset(or8[g:g + DEC, :], 0.0)
            link.step(ins)
            with dve.Fori(0, phG.iters) as it:
                link.enter(it, 16)
                for j in range(len(phG.chunks)):
                    split_lo(dve, phG, it, j + AHEAD)
                    window("middle", (it, 4), j)
                    if j == 5:
                        state_new(it, 0)
                    if j == 6:
                        state_read(it, 0)
                    if j == 12:
                        state_new(it, 1)
                    if j == 14:
                        state_read(it, 1)
                link.leave(phG.iters)

            dve.wait_ge(S["or_ps"], 1)
            for half in range(2):
                last = V.tensor_copy(orS[:, half * 2:half * 2 + 2, :, :].rearrange("p h e b -> p (h e b)"),
                                     X[:, 3 - half, half * 32:half * 32 + 32])
            last.then_inc(S["orS_made"], 1)
            dve.wait_ge(S["t_mean_ps"], 1)
            dve.wait_ge(S["orS_made"], 1)
            for e in range(2):
                last = V.scalar_tensor_tensor(out=orS[:, :, e, :], in0=X[:, 2, 0:32].rearrange("p (h b) -> p h b", h=H_R), scalar=-1.0 / 256.0,
                                              in1=orS[:, :, e, :], op0=ALU.mult, op1=ALU.add)
            last.then_inc(S["t_cen"], 1)
            dve.wait_ge(S["t_std"], 1)
            link.step(V.reciprocal(small[:, 2, 32:64], small[:, 2, 0:32]))
            rec = small[:, 2, 32:64].rearrange("p (h b) -> p h b", h=H_R)
            for e in range(2):
                ins = V.tensor_tensor(orS[:, :, e, :], orS[:, :, e, :], rec, ALU.mult)
            link.step(ins)
            gn = par[:, 96:104].unsqueeze(2).broadcast_to([P, 8, DEC])
            o8 = orS[:, :, :, :].rearrange("p h e b -> p (h e) b")
            link.step(V.tensor_tensor(o8, o8, gn, ALU.mult))
            V.tensor_tensor(o8, o8, sgS[:, :, :, :].rearrange("p h e b -> p (h e) b"), ALU.mult).then_inc(S["t_or"], 1)
            dve.wait_ge(S["t_hi"], 1)
            V.tensor_tensor(orT_lo[:, :, SEQ:T], o8, orT_hi[:, :, SEQ:T].bitcast(F32), ALU.subtract).then_inc(S["t_lo"], 1)

            for j in range(len(phYR.chunks)):
                split_lo(dve, phYR, 0, j + AHEAD)
                window("last", (None, DEC), j)
                if j == 3:
                    dve.wait_ge(S["pnew_made"], DEC)
                    V.tensor_tensor(pdiag[:, :, :], ident[0:8, 0:8].unsqueeze(2).broadcast_to([8, H_F, DEC]),
                                    pnew8[:, :].unsqueeze(1).broadcast_to([8, H_F, DEC]), ALU.mult).then_inc(S["t_diag"], 1)
                if phYR.chunks[j].last:
                    ac, k = phYR.chunks[j].acc, j // 2 * 2
                    group_done(dve, phYR, 0, j)
                    g = gate[:, k:k + 2, 0, :]
                    V.tensor_tensor(g, g, acc2(ac), ALU.mult).then_inc(free[ac], 1)
            dve.wait_ge(S["of_made"], 9)
            dve.wait_ge(S["t_pb_ps"], 1)
            of = small[:, 0, :]
            link.step(V.tensor_tensor(of, X[:, 3, 0:64], vS[:, :, :].rearrange("p h b -> p (h b)"), ALU.mult))
            V.tensor_tensor(of, of, ofS[:, :, :].rearrange("p h b -> p (h b)"), ALU.add).then_inc(S["t_of"], 1)
            dve.wait_ge(S["t_hi"], 2)
            V.tensor_tensor(ofT_lo[:, :, SEQ:T], of.rearrange("p (h b) -> p h b", h=H_F), ofT_hi[:, :, SEQ:T].bitcast(F32), ALU.subtract)\
                .then_inc(S["t_lo"], 1)

            with dve.Fori(0, phYF.iters) as it:
                link.enter(it, 4)
                for j in range(len(phYF.chunks)):
                    split_lo(dve, phYF, it, j + AHEAD)
                    if phYF.chunks[j].last:
                        n = phYF.chunks[j].acc
                        group_done(dve, phYF, it, j)
                        k = ds(it * 4 + n * 2, 2)
                        V.tensor_tensor(gate[:, k, 1, :], gate[:, k, 1, :], acc2(n), ALU.mult).then_inc(free[n], 1)
                        dve.wait_ge(free[n], phYF.group(it, j) + 2)
                        V.tensor_tensor(gate[:, k, 0, :], gate[:, k, 0, :], gate[:, k, 1, :], ALU.add).then_inc(S["mix_made"], 1)
                        dve.wait_ge(S["mix_hi_made"], it * 2 + (n + 1))
                        V.tensor_tensor(mix_lo[:, k, :], gate[:, k, 0, :], mix_hi[:, k, :].bitcast(F32), ALU.subtract)\
                            .then_inc(S["mix_lo_made"], 1)
                link.leave(phYF.iters)

            dve.wait_ge(S["mix_lo_made"], 8)
            link.step(V.memset(usum[:, :, :], 0.0))
            with dve.Fori(0, phO.iters) as it:
                link.enter(it, 8)
                for j in range(len(phO.chunks)):
                    split_lo(dve, phO, it, j + AHEAD)
                    if phO.chunks[j].last:
                        n = phO.chunks[j].acc
                        group_done(dve, phO, it, j)
                        k = it * 4 + n * 2
                        u = uT[:, ds(k, 2), :]
                        V.scalar_tensor_tensor(out=u, in0=hT_hi[:, ds(k, 2), :].bitcast(F32), scalar=ALPHA, in1=acc2(n), op0=ALU.mult, op1=ALU.add)\
                            .then_inc(free[n], 1)
                        dve.wait_ge(free[n], phO.group(it, j) + 2)
                        link.step(V.scalar_tensor_tensor(out=u, in0=hT_lo[:, ds(k, 2), :].bitcast(F32), scalar=ALPHA, in1=u, op0=ALU.mult, op1=ALU.add))
                        ins = V.tensor_tensor(usum[:, :, :], usum[:, :, :], u, ALU.add)
                        if n == 0:
                            link.step(ins)
                        else:
                            ins.then_inc(S["u_made"], 1)
                            dve.wait_ge(S["u_made"], it + 1)
                link.leave(phO.iters)

            def y_rows(q):
                dve.wait_ge(S["yT_ps"], q * 3 + 3)
                if q >= 2:
                    dve.wait_ge(y8_stored[q % 2], 16 * (q // 2))
                V.tensor_copy(ytok8[:, q % 2, :], X[0:DEC, (q * 3 + 2) % 4, :]).then_inc(S["y8_tok"], 1)

            def norm(n, g0):
                dve.wait_ge(S["lnm_ps"], n + 1)
                link.step(V.tensor_scalar(sgt[:, 0, :], X[:, 0, 0:T], 1.0 / D, None, ALU.mult))
                for q in range(4):
                    u = uT[:, q * 4:q * 4 + 4, :]
                    V.tensor_tensor(u, u, sgt[:, 0:1, :].broadcast_to([P, 4, T]), ALU.subtract).then_inc(S["cen_made"], 1)
                dve.wait_ge(S["lnstd_made"], n + 1)
                link.step(V.reciprocal(rstd[:, :], rstd[:, :]))
                dve.wait_ge(S["cen_made"], 4 * n + 4)
                dve.wait_ge(S["sq_made"], 4 * n + 4)
                for q in range(4):
                    u = uT[:, q * 4:q * 4 + 4, :]
                    V.tensor_tensor(u, u, rstd[:, :].unsqueeze(1).broadcast_to([P, 4, T]), ALU.mult).then_inc(S["scaled"], 1)
                    dve.wait_ge(S["scaled"], 4 * n + q + 1)
                    for k in range(q * 4, q * 4 + 2):
                        V.tensor_scalar(uT[:, k, :], uT[:, k, :], par[:, g0 + k:g0 + k + 1], par[:, g0 + 16 + k:g0 + 17 + k], ALU.mult, ALU.add)\
                            .then_inc(S["x1_made"], 1)
                    if n == 0:
                        for k in range(q * 4, q * 4 + 4):
                            dve.wait_ge(S["x1_hi_made"], k + 1)
                            V.tensor_tensor(x1_lo[:, k, :], uT[:, k, :], x1_hi[:, k, :].bitcast(F32), ALU.subtract).then_inc(S["x1_lo_made"], 1)
                    elif q >= 1:
                        y_rows(q - 1)
            norm(0, 32)

            with dve.Fori(0, phP.iters) as it:
                link.enter(it, 8)
                for j in range(len(phP.chunks)):
                    split_lo(dve, phP, it, j + AHEAD)
                    if j % 5 == 4:
                        i = j // 5
                        dve.wait_ge(free[0], phP.group(it, j - 1) + 2)
                        group_done(dve, phP, it, j)
                        V.tensor_tensor(sgt[:, :, :], sgt[:, :, :], acc2(1), ALU.mult).then_inc(free[1], 1)
                        dve.wait_ge(free[1], phP.group(it, j) + 2)
                        u = uT[:, ds(it * 8 + i * 2, 2), :]
                        V.scalar_tensor_tensor(out=u, in0=u, scalar=ALPHA, in1=sgt[:, :, :], op0=ALU.mult, op1=ALU.add).then_inc(S["r_res"], 1)
                link.leave(phP.iters)

            def down_step(ph, it, j, last_half):
                n = ph.chunks[j].acc
                group_done(dve, ph, it, j)
                u = uT[:, ds(it * 4 + n * 2, 2), :]
                V.tensor_tensor(u, u, acc2(n), ALU.add).then_inc(free[n], 1)
                if last_half:
                    dve.wait_ge(free[n], ph.group(it, j) + 2)
                    ins = V.tensor_tensor(usum[:, :, :], usum[:, :, :], u, ALU.add)
                    if n == 0:
                        link.step(ins)
                    else:
                        ins.then_inc(S["u_made"], 1)
                        dve.wait_ge(S["u_made"], it + 5)

            dve.wait_ge(S["r_res"], 9)
            link.step(V.memset(usum[:, :, :], 0.0))
            for half, (up, down) in enumerate(ffn):
                with dve.Fori(0, up.iters) as it:
                    for j in range(len(up.chunks)):
                        split_lo(dve, up, it, j + AHEAD)
                        if j == 7:
                            n_g = it + half * HF2 // 2
                            dve.wait_ge(free[0], up.group(it, 3) + 2)
                            group_done(dve, up, it, j)
                            V.tensor_tensor(gact[:, :, :], gact[:, :, :], acc2(1), ALU.mult).then_inc(free[1], 1)
                            dve.wait_ge(free[1], up.group(it, j) + 2)
                            dve.sem_inc(S["g_made"], 1)
                            dve.wait_ge(S["g_hi_made"], n_g + 1)
                            V.tensor_tensor(g_lo[:, ds(it * 2, 2), :], gact[:, :, :], g_hi[:, ds(it * 2, 2), :].bitcast(F32), ALU.subtract)\
                                .then_inc(S["g_lo_made"], 1)
                with dve.Fori(0, down.iters) as it:
                    link.enter(it, 4)
                    for j in range(len(down.chunks)):
                        split_lo(dve, down, it, j + AHEAD)
                        if down.chunks[j].last:
                            down_step(down, it, j, half == 1)
                    link.leave(down.iters)
            for j in range(len(phLast.chunks)):
                if j + AHEAD < len(phLast.chunks):
                    split_lo(dve, phLast, 0, j + AHEAD)
                if phLast.chunks[j].last:
                    n = phLast.chunks[j].acc
                    group_done(dve, phLast, 0, j)
                    u = uT[:, 12 + n * 2:14 + n * 2, :]
                    V.tensor_tensor(u, u, acc2(n), ALU.add).then_inc(free[n], 1)
                    dve.wait_ge(free[n], phLast.group(0, j) + 2)
                    ins = V.tensor_tensor(usum[:, :, :], usum[:, :, :], u, ALU.add)
                    if n == 0:
                        link.step(ins)
                    else:
                        ins.then_inc(S["u_made"], 1)
            norm(1, 64)
            y_rows(3)

        @block.gpsimd
        def _(pool):
            for k in range(DT):
                pool.wait_ge(S["h_hi"], k + 1)
                nc.gpsimd.tensor_tensor(hT_lo[:, k, :], h32[:, k, :], hT_hi[:, k, :].bitcast(F32), ALU.subtract).then_inc(S["h_lo"], 1)
            pool.dma_start(ptab[:, :], a["page_table"]).then_inc(S["ptab_in"], 16)
            pool.wait_ge(S["ptab_in"], 16)
            with pool.Fori(0, DEC * NPG) as i:
                number = pool.value_load(ptab[0:1, ds(i, 1)], min_val=0, max_val=NPOOL - 1)
                pool.dma_start(Lc[:, ds(i, 1), :].rearrange("s o h -> s (o h)"), a["cache_logf"][ds(number, 1)].rearrange("o s h -> s (o h)"))\
                    .then_inc(S["past_in"], 16)
            pool.wait_ge(S["logf_made"], 2)
            pool.dma_start(a["fox_logf_prompt"].rearrange("(t p) h -> p t h", p=P), logf_tok[:, :, :]).then_inc(S["st_stored"], 16)
            pool.dma_start(a["fox_logf_sample"], logfS[:, :]).then_inc(S["st_stored"], 16)
            def store_values(it):
                cols = slice(it * 512, it * 512 + 512)
                pool.wait_ge(S["f_vtok_sb"], it * 2 + 2)
                pool.dma_start(a["fox_v_prompt"].rearrange("(t p) c -> p t c", p=P)[:, :, cols], vtok[:, :, :]).then_inc(S["f_store_v"], 16)
                pool.dma_start(a["fox_v_sample"][:, cols], vs8[:, :]).then_inc(S["f_store_v"], 16)

            for it in range(phF.iters):
                cols = slice(it * 512, it * 512 + 512)
                pool.wait_ge(S["f_ktok_sb"], it * 2 + 2)
                pool.dma_start(a["fox_k_prompt"].rearrange("(t p) c -> p t c", p=P)[:, :, cols], ktok[:, :, :]).then_inc(S["f_store_k"], 16)
                pool.dma_start(a["fox_k_sample"][:, cols], kqs[:, 0, :]).then_inc(S["f_store_k"], 16)
                pool.dma_start(q_rows[:, cols], kqs[:, 1, :]).then_inc(S["f_store_k"], 16)
                if it == 0:
                    store_values(0)
            pool.wait_ge(S["f_store_k"], 96)
            pool.wait_ge(S["decay_ps"], 1)

            def load_page(sort, slot, n):
                kind, p = ORDER[sort][n]
                if n >= PAGES:
                    (used, q), back = ORDER[sort][n - PAGES], 0
                elif sort == "first":
                    used = None
                else:
                    (used, q), back = ORDER["first" if slot[0] is None and slot[1] == 1 else "middle"][n - PAGES], 1
                if used == "key":
                    pool.wait_ge(S["page_used"], line(slot, NPG * H_F, (q + 1 - NPG * back) * H_F + HEADS))
                elif used == "value":
                    pool.wait_ge(S["pv_ps"], line(slot, NPG, q + 2 - NPG * (back + 1)))
                if slot[0] is not None:
                    pool.sem_inc(S["pool_step"], 1)
                index = line(slot, NPG, p - (NPG if kind == "value" else 0))
                number = pool.value_load(ptab[0:1, ds(index, 1)], min_val=0, max_val=NPOOL - 1)
                pool.dma_start(page[:, n % PAGES, :], a["cache_k" if kind == "key" else "cache_v"][ds(number, 1)].rearrange("o s c -> s (o c)"))\
                    .then_inc(page_in[n % PAGES], 16)

            def load_query(slot):
                pool.wait_ge(S["page_used"], line(slot, NPG * H_F, HEADS))
                if slot[0] is not None:
                    pool.sem_inc(S["pool_step"], 1)
                pool.dma_start(qbc[:, :], q_rows[ds(line(slot, 1, 0), 1), :].partition_broadcast(P)).then_inc(S["q_in"], 16)

            for m in range(4):
                sort, slot, cols = "middle" if m else "first", (None, m), slice(m // 2 * 512, m // 2 * 512 + 512)
                load_query(slot)
                for n in range(len(ORDER[sort])):
                    load_page(sort, slot, n)
                    if m == 0 and n == 3:
                        store_values(1)
                    if m % 2 == 1 and n == 8:
                        pool.wait_ge(S["r_v_sb"], m + 1)
                        pool.dma_start(v_rows[:, cols], vr8[:, :]).then_inc(S["r_store_v"], 16)
                    if m % 2 == 1 and n == 11:
                        pool.wait_ge(S["r_s_sb"], m + 1)
                        pool.dma_start(a["ret_state_prompt"][m - 1:m + 1].rearrange("h (d p) e -> p (h d) e", p=P),
                                       stR[:, :, :].rearrange("p h (d e) -> p (h d) e", d=2)).then_inc(S["r_store_s"], 16)

            def load_state(it, n):
                k = it * 2 + n
                pool.wait_ge(S["st_ps"], k + 1)
                pool.wait_ge(S["st_stored"], k * 16 + 32)
                pool.sem_inc(S["pool_step"], 1)
                pool.dma_start(stateS[:, :, :, :].rearrange("p h d e -> p (h d) e"),
                               a["state_ret"][ds(k, 1)].rearrange("o h (d p) e -> p (o h d) e", p=P)).then_inc(S["st_in"], 16)

            def load_values(it, n):
                k = it * 2 + n
                pool.dma_start(vbc[:, :, :].rearrange("p h e -> p (h e)"), v_rows[ds(k, 1), :].partition_broadcast(P)).then_inc(S["vb_in"], 16)

            def store_state(it, n):
                k = it * 2 + n
                pool.wait_ge(S["st_new"], k + 1)
                pool.sem_inc(S["pool_step"], 1)
                pool.dma_start(a["ret_state_sample"][ds(k, 1)].rearrange("o h (d p) e -> p (o h d) e", p=P),
                               stateS[:, :, :, :].rearrange("p h d e -> p (h d) e")).then_inc(S["st_stored"], 16)

            with pool.Fori(0, phG.iters) as it:
                load_query((it, 4))
                for n in range(2 * NPG):
                    if n == 2:
                        pool.wait_ge(S["r_store_v"], 32)
                        pool.wait_ge(S["r_store_s"], 32)
                        pool.wait_ge(S["r_lo"], 4)
                        load_state(it, 0)
                    if n == 4:
                        load_values(it, 0)
                    if n == 8:
                        store_state(it, 0)
                    if n == 10:
                        load_state(it, 1)
                    if n == 12:
                        load_values(it, 1)
                    load_page("middle", (it, 4), n)
                store_state(it, 1)
            for n in range(NPG):
                load_page("last", (None, DEC), n)

            pool.wait_ge(S["f_store_k"], 96)
            pool.wait_ge(S["f_store_v"], 64)
            pool.wait_ge(S["r_store_s"], 32)
            pool.wait_ge(S["r_store_v"], 32)
            pool.wait_ge(S["st_stored"], 32 + 16 * DEC)



SLAB_BASE = 16512


def kernel(**inputs):
    import concourse.bacc as _bacc
    from concourse.bass_utils import run_bass_kernel_spmd as _run

    x = {k: np.asarray(v) for k, v in inputs.items()}
    _, SEQ, D = x["x_prompt"].shape
    DEC, NPG = x["page_table"].shape
    NPOOL, PAGE = x["cache_k"].shape[1:3]
    H_F, D_F = x["cache_k"].shape[3:]
    _, _, H_R, DK, DV = x["state_ret"].shape
    dims = {"D": D, "SEQ": SEQ, "DEC": DEC, "NPG": NPG, "NPOOL": NPOOL, "H_R": H_R, "H_F": H_F, "D_FF": x["w1"].shape[2]}
    blob, where, gammas = shape_constants(SEQ, DEC, NPG * PAGE, H_R)
    shaped = {
        "x_prompt": (SEQ, D), "x_sample": (DEC, D), "state_ret": (DEC, H_R, DK, DV),
        "cache_k": (NPOOL, PAGE, H_F * D_F), "cache_v": (NPOOL, PAGE, H_F * D_F), "cache_logf": (NPOOL, PAGE, H_F),
        "page_table": (1, DEC * NPG), "p_prompt": (SEQ, x["p_prompt"].shape[-1]), "p_sample": (DEC, x["p_sample"].shape[-1]),
        "gn_g": (H_R * DV,),
    }
    nc = _bacc.Bacc("TRN2", target_bir_lowering=False, num_devices=1)
    arrays, aps = {}, {}
    for name, v in {**x, "shape_constants": blob}.items():
        if name in shaped:
            v = v.reshape(shaped[name])
        elif v.ndim == 3 or name in ("b_f", "ln1_g", "ln1_b", "ln2_g", "ln2_b"):
            v = v.reshape(v.shape[1:])
        arrays["in_" + name] = np.ascontiguousarray(v)
        aps[name] = nc.dram_tensor("in_" + name, v.shape, mybir.dt.from_np(v.dtype), kind="ExternalInput").ap()
    outs = {
        "y_prompt": ((SEQ, D), (1, SEQ, D)), "y_sample": ((DEC, D), (DEC, 1, D)),
        "ret_state_prompt": ((H_R, DK, DV), (1, 1, H_R, DK, DV)),
        "fox_k_prompt": ((SEQ, H_F * D_F), (1, 1, SEQ, H_F, D_F)), "fox_v_prompt": ((SEQ, H_F * D_F), (1, 1, SEQ, H_F, D_F)),
        "fox_logf_prompt": ((SEQ, H_F), (1, 1, SEQ, H_F)),
        "ret_state_sample": ((DEC, H_R, DK, DV), (1, DEC, H_R, DK, DV)),
        "fox_k_sample": ((DEC, H_F * D_F), (1, DEC, 1, H_F, D_F)), "fox_v_sample": ((DEC, H_F * D_F), (1, DEC, 1, H_F, D_F)),
        "fox_logf_sample": ((DEC, H_F), (1, DEC, 1, H_F)),
    }
    for name, (shape, _) in outs.items():
        aps[name] = nc.dram_tensor("out_" + name, shape, F32, kind="ExternalOutput").ap()
    layer_kernel(nc, aps, where, gammas, dims)
    r = _run(nc, [arrays], core_ids=[0])
    return tuple(r.results[0]["out_" + name].reshape(full) for name, (_, full) in outs.items())
```
